# Optimizing a Trainium2 kernel written in Bass

```python
import jax, jax.numpy as jnp
from jax import lax
import numpy as np

D_MODEL = 1024
BATCH = 1
SEQ = 1024
DEPTH = 1

HEAD_DIM = 64
N_Q_HEADS = 8
N_KV_HEADS = 2
GROUP = N_Q_HEADS // N_KV_HEADS
ATTN_WIDTH = N_Q_HEADS * HEAD_DIM
KV_WIDTH = N_KV_HEADS * HEAD_DIM
WINDOW = 128
BLOCK = 128
ROPE_THETA = 10000.0
LRU_WIDTH = D_MODEL // 2
LRU_HEADS = 8
LRU_BLOCK = LRU_WIDTH // LRU_HEADS
LRU_C = 8.0
CONV_WIDTH = 4
N_EXPERTS = 32
TOP_K = 4
D_EXPERT = D_MODEL
SWIGLU_LIMIT = 7.0
SWIGLU_ALPHA = 1.702
MOE_CHUNK = 128
NORM_EPS = 1e-6
NEG_INF = -1e30
IN_SPLITS = (ATTN_WIDTH, KV_WIDTH, KV_WIDTH, LRU_WIDTH, LRU_WIDTH, D_MODEL, D_MODEL)
IN_WIDTH = sum(IN_SPLITS)

kernel_name = "hybrid_swa_sink_rglru_moe_block"

def rmsnorm(x, g):
    x32 = x.astype(jnp.float32)
    y = x32 * lax.rsqrt(jnp.mean(x32 * x32, axis=-1, keepdims=True) + NORM_EPS)
    return (y * g.astype(jnp.float32)).astype(x.dtype)

def split_cols(p):
    outs, o = [], 0
    for w in IN_SPLITS:
        outs.append(p[..., o:o + w])
        o += w
    return outs

def rope(t, positions):
    hd = t.shape[-1]
    inv_freq = 1.0 / (ROPE_THETA ** (jnp.arange(0, hd, 2, dtype=jnp.float32) / hd))
    ang = positions[..., None].astype(jnp.float32) * inv_freq
    cos = jnp.cos(ang)[:, :, None, :]
    sin = jnp.sin(ang)[:, :, None, :]
    t32 = t.astype(jnp.float32)
    t1, t2 = t32[..., :hd // 2], t32[..., hd // 2:]
    out = jnp.concatenate([t1 * cos - t2 * sin, t2 * cos + t1 * sin], axis=-1)
    return out.astype(t.dtype)

def sliding_window_attention(q, k, v, sinks):
    bsz, s = q.shape[0], q.shape[1]
    nb = s // BLOCK
    qb = q.reshape(bsz, nb, BLOCK, N_KV_HEADS, GROUP, HEAD_DIM)

    def with_prev(t):
        tb = t.reshape(bsz, nb, BLOCK, N_KV_HEADS, HEAD_DIM)
        prev = jnp.concatenate([jnp.zeros_like(tb[:, :1]), tb[:, :-1]], axis=1)
        return jnp.concatenate([prev, tb], axis=2)

    kk, vv = with_prev(k), with_prev(v)
    scores = jnp.einsum('bnqhgd,bnkhd->bhgnqk', qb, kk).astype(jnp.float32) * (HEAD_DIM ** -0.5)
    blk = jnp.arange(nb)[:, None, None]
    qpos = blk * BLOCK + jnp.arange(BLOCK)[None, :, None]
    kpos = (blk - 1) * BLOCK + jnp.arange(2 * BLOCK)[None, None, :]
    diff = qpos - kpos
    mask = (diff >= 0) & (diff < WINDOW) & (kpos >= 0)
    scores = jnp.where(mask, scores, NEG_INF)
    sink = sinks.astype(jnp.float32).reshape(N_KV_HEADS, GROUP)[None, :, :, None, None, None]
    m = jnp.maximum(jnp.max(scores, axis=-1, keepdims=True), sink)
    p = jnp.exp(scores - m)
    p = p / (jnp.sum(p, axis=-1, keepdims=True) + jnp.exp(sink - m))
    o = jnp.einsum('bhgnqk,bnkhd->bnqhgd', p.astype(v.dtype), vv)
    return o.reshape(bsz, s, ATTN_WIDTH)

def causal_depthwise_conv(xr, w, b):
    y = lax.conv_general_dilated(xr, w[:, None, :].astype(xr.dtype), window_strides=(1,),
                                 padding=[(CONV_WIDTH - 1, 0)],
                                 dimension_numbers=('NWC', 'WIO', 'NWC'),
                                 feature_group_count=LRU_WIDTH)
    return y + b

def rg_lru(xb, w_rg, b_rg, w_ig, b_ig, lam):
    bsz, s, _ = xb.shape
    x32 = xb.astype(jnp.float32)
    xh = x32.reshape(bsz, s, LRU_HEADS, LRU_BLOCK)
    r = jax.nn.sigmoid(jnp.einsum('bshi,hij->bshj', xh, w_rg.astype(jnp.float32)).reshape(bsz, s, LRU_WIDTH) + b_rg.astype(jnp.float32))
    i = jax.nn.sigmoid(jnp.einsum('bshi,hij->bshj', xh, w_ig.astype(jnp.float32)).reshape(bsz, s, LRU_WIDTH) + b_ig.astype(jnp.float32))
    log_a = -LRU_C * r * jax.nn.softplus(-lam.astype(jnp.float32))
    a = jnp.exp(log_a)
    u = jnp.sqrt(-jnp.expm1(2.0 * log_a)) * (i * x32)

    def combine(c1, c2):
        a1, b1 = c1
        a2, b2 = c2
        return a1 * a2, a2 * b1 + b2

    _, h = lax.associative_scan(combine, (a, u), axis=1)
    return h.astype(xb.dtype)

def mixer(h, positions, w_in, conv_w, conv_b, w_rg, b_rg, w_ig, b_ig, lru_lambda,
          attn_sinks, w_attn_o, w_lru_o, w_out):
    bsz, s, _ = h.shape
    q, k, v, xr, yr, ga, gl = split_cols(h @ w_in)
    q = rope(q.reshape(bsz, s, N_Q_HEADS, HEAD_DIM), positions)
    k = rope(k.reshape(bsz, s, N_KV_HEADS, HEAD_DIM), positions)
    v = v.reshape(bsz, s, N_KV_HEADS, HEAD_DIM)
    y_attn = sliding_window_attention(q, k, v, attn_sinks) @ w_attn_o
    xr = causal_depthwise_conv(xr, conv_w, conv_b)
    y_lru = (rg_lru(xr, w_rg, b_rg, w_ig, b_ig, lru_lambda) * jax.nn.gelu(yr)) @ w_lru_o
    merged = jax.nn.sigmoid(ga) * y_attn + jax.nn.sigmoid(gl) * y_lru
    return merged @ w_out

def moe(h, w_router, b_router, w_gate_up, b_gate_up, w_down, b_down):
    bsz, s, d = h.shape
    n = bsz * s
    t = h.reshape(n, d)
    logits = (t @ w_router + b_router).astype(jnp.float32)
    top_val, top_idx = lax.top_k(logits, TOP_K)
    gate = jax.nn.softmax(top_val, axis=-1)
    nk = n * TOP_K
    flat_e = top_idx.reshape(-1).astype(jnp.int32)
    flat_tok = jnp.repeat(jnp.arange(n, dtype=jnp.int32), TOP_K)
    flat_w = gate.reshape(-1)
    order = jnp.argsort(flat_e)
    se = flat_e[order]
    counts = jnp.zeros((N_EXPERTS,), jnp.int32).at[flat_e].add(1)
    starts = jnp.cumsum(counts) - counts
    pcounts = (counts + MOE_CHUNK - 1) // MOE_CHUNK * MOE_CHUNK
    pends = jnp.cumsum(pcounts)
    pstarts = pends - pcounts
    dest = pstarts[se] + (jnp.arange(nk, dtype=jnp.int32) - starts[se])
    n_chunks = -(-nk // MOE_CHUNK) + N_EXPERTS
    n_slots = n_chunks * MOE_CHUNK
    slot_tok = jnp.zeros((n_slots,), jnp.int32).at[dest].set(flat_tok[order])
    slot_w = jnp.zeros((n_slots,), jnp.float32).at[dest].set(flat_w[order])
    chunk_start = jnp.arange(n_chunks, dtype=jnp.int32) * MOE_CHUNK
    chunk_e = jnp.clip(jnp.searchsorted(pends, chunk_start, side='right'), 0, N_EXPERTS - 1)
    xs = t[slot_tok].reshape(n_chunks, MOE_CHUNK, d)

    def expert_block(args):
        xc, e = args
        gu = xc @ w_gate_up[e] + b_gate_up[e]
        g, u = gu[:, :D_EXPERT], gu[:, D_EXPERT:]
        g = jnp.minimum(g, SWIGLU_LIMIT)
        u = jnp.clip(u, -SWIGLU_LIMIT, SWIGLU_LIMIT)
        act = (u + 1.0) * (g * jax.nn.sigmoid(SWIGLU_ALPHA * g))
        return act @ w_down[e] + b_down[e]

    ys = lax.map(expert_block, (xs, chunk_e)).reshape(n_slots, d)
    out = jnp.zeros((n, d), jnp.float32).at[slot_tok].add(ys.astype(jnp.float32) * slot_w[:, None])
    return out.astype(h.dtype).reshape(bsz, s, d)

def setup_inputs(seed: int = 0) -> dict:
    key = jax.random.key(seed)
    ks = jax.random.split(key, 24)
    f32 = jnp.float32
    nrm = lambda k, shape, scale: jax.random.normal(k, shape, f32) * scale
    a0 = jax.random.uniform(ks[9], (DEPTH, LRU_WIDTH), f32, 0.9, 0.999)
    s0 = a0 ** (1.0 / LRU_C)
    lru_lambda = jnp.log(s0) - jnp.log1p(-s0)
    return {
        "x": nrm(ks[0], (BATCH, SEQ, D_MODEL), 1.0),
        "positions": jnp.broadcast_to(jnp.arange(SEQ, dtype=jnp.int32), (BATCH, SEQ)),
        "norm_mix_g": 1.0 + nrm(ks[1], (DEPTH, D_MODEL), 0.02),
        "w_in": nrm(ks[2], (DEPTH, D_MODEL, IN_WIDTH), D_MODEL ** -0.5),
        "conv_w": nrm(ks[3], (DEPTH, CONV_WIDTH, LRU_WIDTH), CONV_WIDTH ** -0.5),
        "conv_b": nrm(ks[4], (DEPTH, LRU_WIDTH), 0.01),
        "w_rg": nrm(ks[5], (DEPTH, LRU_HEADS, LRU_BLOCK, LRU_BLOCK), LRU_BLOCK ** -0.5),
        "b_rg": nrm(ks[6], (DEPTH, LRU_WIDTH), 0.01),
        "w_ig": nrm(ks[7], (DEPTH, LRU_HEADS, LRU_BLOCK, LRU_BLOCK), LRU_BLOCK ** -0.5),
        "b_ig": nrm(ks[8], (DEPTH, LRU_WIDTH), 0.01),
        "lru_lambda": lru_lambda,
        "attn_sinks": nrm(ks[10], (DEPTH, N_Q_HEADS), 0.5),
        "w_attn_o": nrm(ks[11], (DEPTH, ATTN_WIDTH, D_MODEL), ATTN_WIDTH ** -0.5),
        "w_lru_o": nrm(ks[12], (DEPTH, LRU_WIDTH, D_MODEL), LRU_WIDTH ** -0.5),
        "w_out": nrm(ks[13], (DEPTH, D_MODEL, D_MODEL), D_MODEL ** -0.5),
        "norm_ffn_g": 1.0 + nrm(ks[14], (DEPTH, D_MODEL), 0.02),
        "w_router": nrm(ks[15], (DEPTH, D_MODEL, N_EXPERTS), D_MODEL ** -0.5),
        "b_router": nrm(ks[16], (DEPTH, N_EXPERTS), 0.01),
        "w_gate_up": nrm(ks[17], (DEPTH, N_EXPERTS, D_MODEL, 2 * D_EXPERT), D_MODEL ** -0.5),
        "b_gate_up": nrm(ks[18], (DEPTH, N_EXPERTS, 2 * D_EXPERT), 0.01),
        "w_down": nrm(ks[19], (DEPTH, N_EXPERTS, D_EXPERT, D_MODEL), D_EXPERT ** -0.5),
        "b_down": nrm(ks[20], (DEPTH, N_EXPERTS, D_MODEL), 0.01),
        "norm_final_g": 1.0 + nrm(ks[21], (D_MODEL,), 0.02),
    }

def reference(x, positions, norm_mix_g, w_in, conv_w, conv_b, w_rg, b_rg, w_ig, b_ig,
              lru_lambda, attn_sinks, w_attn_o, w_lru_o, w_out, norm_ffn_g, w_router,
              b_router, w_gate_up, b_gate_up, w_down, b_down, norm_final_g):
    for l in range(DEPTH):
        h = rmsnorm(x, norm_mix_g[l])
        x = x + mixer(h, positions, w_in[l], conv_w[l], conv_b[l], w_rg[l], b_rg[l],
                      w_ig[l], b_ig[l], lru_lambda[l], attn_sinks[l], w_attn_o[l],
                      w_lru_o[l], w_out[l])
        h = rmsnorm(x, norm_ffn_g[l])
        x = x + moe(h, w_router[l], b_router[l], w_gate_up[l], b_gate_up[l],
                    w_down[l], b_down[l])
    return rmsnorm(x, norm_final_g)


_drawn_inputs = setup_inputs


def setup_inputs(seed=0):
    import zlib

    import numpy as np

    out = dict(_drawn_inputs(seed))
    spreads = {}
    factors = {'b_rg': 22.093,
     'b_ig': 7.015,
     'attn_sinks': 8.0,
     'b_gate_up': 8.0,
     'b_down': 8.0,
     'norm_final_g': 7.556}
    for name, (base, spread) in spreads.items():
        noise = np.random.default_rng([zlib.crc32(name.encode()), seed]).standard_normal(out[name].shape)
        drawn = base * np.exp(spread * noise) if base else spread * noise
        out[name] = __import__('jax').numpy.asarray(drawn.astype(out[name].dtype))
    for name, factor in factors.items():
        out[name] = (out[name] * factor).astype(out[name].dtype)
    return out
```

```python
import concourse.bass as bass
from concourse import mybir
from contextlib import ExitStack

SEQ, D = 1024, 1024
P = 128
NT = SEQ // P
KD = D // P
HALF = 512
N_Q, N_KV, HD = 8, 2, 64
GROUP = N_Q // N_KV
QW, KVW, LW = N_Q * HD, N_KV * HD, D // 2
LM = LW // P
CONV = 4
NE, TOPK = 32, 4
MAXC = SEQ * TOPK // P + NE
NU = 6
SLOTS = 8
TAIL = 32
QUART = P // TAIL
QC = D // QUART
UNIT = KD * HALF
SHIFT = 4
FAR = 4096
NEG_INF = -1e30
LRU_C = 8.0
LIMIT, ALPHA = 7.0, 1.702
EPS = 1e-6
NMETA = 6
A_COLS = 6528
TWO_PI_PARTS = (6.28125, 0.00193500518798828125, 3.0199159819562e-07)
MAGIC = 12582912.0


def hybrid_decoder_block(nc, x, positions, norm_mix_g, w_in, conv_w, conv_b, w_rg, b_rg, w_ig, b_ig,
                         lru_lambda, attn_sinks, w_attn_o, w_lru_o, w_out, norm_ffn_g, w_router, b_router,
                         w_gate_up, b_gate_up, w_down, b_down, norm_final_g, inv_freq, out):
    f32, bf16, i32, u32 = mybir.dt.float32, mybir.dt.bfloat16, mybir.dt.int32, mybir.dt.uint32
    ALU, ACT = mybir.AluOpType, mybir.ActivationFunctionType
    AX = mybir.AxisListType.X
    ds = bass.ds

    h2_rows = nc.dram_tensor("h2_rows", [SEQ, D], f32, kind="Internal").ap()
    acc_rows = nc.dram_tensor("acc_rows", [SEQ, D], f32, kind="Internal").ap()

    x_t = x[0].rearrange("(t p) d -> t p d", p=P)
    out_t = out[0].rearrange("(t p) d -> t p d", p=P)
    h2_t = h2_rows.rearrange("(t p) d -> t p d", p=P)
    acc_t = acc_rows.rearrange("(t p) d -> t p d", p=P)
    w_in_v = w_in[0].rearrange("(k p) n -> p k n", p=P)
    OFF_Q, OFF_KV, OFF_XR = 0, QW, QW + 2 * KVW
    OFF_YR, OFF_GA = OFF_XR + LW, OFF_XR + 2 * LW
    OFF_GL = OFF_GA + D
    w_out_v = w_out[0].rearrange("(k p) n -> p k n", p=P)
    wgu_v = w_gate_up[0].rearrange("e (k p) n -> p e k n", p=P)
    wdn_v = w_down[0].rearrange("e (k p) n -> p e k n", p=P)

    ctx = ExitStack()
    with ctx:
        def sb(name, shape, dt=f32):
            return ctx.enter_context(nc.sbuf_tensor(name, shape, dt))

        def sem(name):
            return ctx.enter_context(nc.semaphore(name))

        ring = sb("ring", [P, SLOTS * UNIT])
        region_m = sb("region_m", [P, LM * (SEQ + 3) + LM * SEQ])
        region_s = sb("region_s", [P, LM * SEQ])
        region_a = sb("region_a", [P, A_COLS])

        def half_slot(n, count=1):
            return ring[:, n * UNIT // 2:(n + count) * UNIT // 2]

        def unit_view(ap, k):
            return ap.rearrange("p (k n) -> p k n", k=k)

        hT = unit_view(ring[:, 4 * UNIT:6 * UNIT], KD)
        oT = unit_view(ring[:, 6 * UNIT:7 * UNIT], GROUP)
        lruT = unit_view(ring[:, 7 * UNIT:8 * UNIT], LM)
        wxr_sb, wyr_sb = unit_view(half_slot(0, 2), KD), unit_view(half_slot(2, 2), KD)
        wq_sb, wkv_sb = unit_view(half_slot(4, 2), KD), unit_view(half_slot(6), KD)
        wao_sb, wlo_sb = unit_view(half_slot(0, 2), GROUP), unit_view(half_slot(2, 2), LM)
        ga_sb = [unit_view(half_slot(h), KD) for h in (7, 4, 7, 4)]
        gl_sb = [unit_view(half_slot(h), KD) for h in (6, 5, 6, 5)]
        wo_sb = [unit_view(half_slot(6, 2), KD), unit_view(half_slot(4, 2), KD)]
        bd = half_slot(7)[:, 0:2 * LM * P].rearrange("p (g m n) -> p g m n", g=2, m=LM)

        mask_first = half_slot(7)[:, 1024:1024 + 2 * P]
        cos = half_slot(7)[:, 1280:1280 + NT * 32].rearrange("p (t d) -> p t d", t=NT)
        sin = half_slot(7)[:, 1536:1536 + NT * 32].rearrange("p (t d) -> p t d", t=NT)

        xin = unit_view(region_m[:, 0:NT * D], NT)
        xr = unit_view(region_m[:, 0:LM * (SEQ + 3)], LM)
        xc = unit_view(region_m[:, LM * (SEQ + 3):LM * (SEQ + 3) + LM * SEQ], LM)
        merged = unit_view(region_m[:, 0:KD * SEQ], KD)
        rows_g, rowsT = region_m[:, 0:D], region_m[:, D:2 * D]
        gclip = unit_view(region_m[:, 2 * D:3 * D], 2)
        uclip = unit_view(region_m[:, 3 * D:4 * D], 2)
        gsig = unit_view(region_m[:, 4 * D:5 * D], 2)
        actT, yrow = region_m[:, 5 * D:6 * D], region_m[:, 6 * D:7 * D]

        igate = unit_view(region_s[:, :], LM)
        bias3 = region_s[:, 0:1536].bitcast(bf16)
        place = [ring[:, (i + SHIFT) % SLOTS * UNIT:((i + SHIFT) % SLOTS + 1) * UNIT] for i in range(NU)]
        wu = [unit_view(p_, KD) for p_ in place]
        onehot = region_s[:, 1536:2048].bitcast(bf16).rearrange("p (t s) -> p t s", t=NT)
        sel = region_s[:, 2048:4096].bitcast(bf16)

        at = [0]

        def take(n):
            at[0] += n
            assert at[0] <= A_COLS, at[0]
            return region_a[:, at[0] - n:at[0]]

        qk = take((N_Q + N_KV) * HD).rearrange("p (h d) -> p h d", d=HD)
        ropa = take((N_Q + N_KV) * HD // 2).rearrange("p (h d) -> p h d", d=HD // 2)
        ropb = take((N_Q + N_KV) * HD // 2).rearrange("p (h d) -> p h d", d=HD // 2)
        qT = take(GROUP * P).rearrange("p (h q) -> p h q", h=GROUP)
        kT = take((NT + 1) * P)
        vrow = take(4 * P).rearrange("p (b d) -> p b d", b=4)
        prob = [take(GROUP * 2 * P).rearrange("p (h k) -> p h k", h=GROUP) for _ in range(N_KV)]
        pT = take(2 * GROUP * P)
        at[0] = 0
        sgate = [[take(HALF) for _ in range(2)] for _ in range(2)]
        part_a, part_b = take(HALF), take(HALF)
        bstage = take(3 * D)
        at[0] = 0
        xb = [take(D), take(D)]
        h2 = [take(D), take(D)]
        h2T, gffn = take(D), take(D)
        logit = take(NT * NE).rearrange("p (t e) -> p t e", t=NT)
        top_v = take(NT * 8).rearrange("p (t k) -> p t k", t=NT)
        top_i = take(NT * 8).bitcast(u32).rearrange("p (t k) -> p t k", t=NT)
        at[0] = 0
        iota_s = take(SEQ)
        rank = take(NE * NT).rearrange("p (e t) -> p e t", e=NE)
        meta = take(NE * NT * NMETA // 2).bitcast(bf16)
        oh = take(NE * NT).rearrange("p (t e) -> p t e", t=NT)
        ohg = take(NE * NT).rearrange("p (t e) -> p t e", t=NT)
        mask_d = take(NE * NT).rearrange("p (t e) -> p t e", t=NT)
        gate_d = take(NE * NT).rearrange("p (t e) -> p t e", t=NT)
        gate_r = take(NE * NT).rearrange("p (t e) -> p t e", t=NT)
        mask_b = take(NE * NT // 2).bitcast(bf16).rearrange("p (t e) -> p t e", t=NT)
        gfin = take(D)
        top_f = take(NT * 8).rearrange("p (t k) -> p t k", t=NT)
        gate4 = take(NT * TOPK).rearrange("p (t k) -> p t k", t=NT)
        gsum = take(NT)
        cnt, nch, cinc, cexc = (take(NE) for _ in range(4))
        tab_f = take(3 * (MAXC + 1)).rearrange("p (q j) -> p q j", q=3)
        assert at[0] <= 6 * D
        tcmp = region_m[:, 0:(MAXC + 1) * NE].rearrange("p (j e) -> p j e", e=NE)
        tcmp2 = region_m[:, 3 * D:3 * D + (MAXC + 1) * NE].rearrange("p (j e) -> p j e", e=NE)
        fin = [ring[:, t * D:(t + 1) * D] for t in range(NT)]
        fjunk = ring[:, NT * D:(NT + 1) * D]

        ident = sb("ident", [P, P])
        mask = sb("mask", [P, 2 * P])
        wrt = sb("wrt", [P, KD, NE])
        ones_b, tri_b = sb("ones_b", [P, P], bf16), sb("tri_b", [P, P], bf16)
        iota_e = sb("iota_e", [P, NE])
        iota_j = sb("iota_j", [P, MAXC + 1])
        iota_p, iota_t = sb("iota_p", [P, 1]), sb("iota_t", [P, NT])
        brt = sb("brt", [P, NE])
        eps = sb("eps", [P, 1])
        gmix = sb("gmix", [P, KD])
        pos_i, pos_f = sb("pos_i", [P, NT], i32), sb("pos_f", [P, NT])
        freq = sb("freq", [P, HD // 2])
        convw, convb = sb("convw", [P, CONV, LM]), sb("convb", [P, LM])
        brg, big, lam = sb("brg", [P, LM]), sb("big", [P, LM]), sb("lam", [P, LM])
        clam = sb("clam", [P, 6, LM])
        sink = sb("sink", [P, N_Q])
        ssq, rms, rinv = sb("ssq", [P, 3, NT]), sb("rms", [P, 3, NT]), sb("rinv", [P, 3, NT])
        mx, negm, sume, esink, rden = (sb(n, [P, N_Q]) for n in ("mx", "negm", "sume", "esink", "rden"))
        chunk_e, chunk_c = sb("chunk_e", [P, MAXC + 1], i32), sb("chunk_c", [P, MAXC + 1], i32)
        ends = sb("ends", [P, NE], i32)
        meta_s = sb("meta_s", [P, NMETA])
        row_f, w_next, w_cur = sb("row_f", [P, 3]), sb("w_next", [P, 2]), sb("w_cur", [P, 1])
        row_next, row_cur = sb("row_next", [P, 3], i32), sb("row_cur", [P, 2], i32)
        chunk_tail = sb("chunk_tail", [P, MAXC + 1], i32)
        quart = sb("quart", [P, 1])
        sel_cur = sb("sel_cur", [P, P], bf16)
        psum = ctx.enter_context(nc.psum_tensor("psum", [P, 8 * HALF], f32))

        def bank(n, count=1):
            return psum[:, n * HALF:(n + count) * HALF]

        x_in = [sem(f"x_in{t}") for t in range(NT)]
        consts_in, small_built = sem("consts_in"), sem("small_built")
        ssq_done, rms_done, rinv_done, xn_done, xT_done, hT_done = (
            sem(n) for n in ("ssq_done", "rms_done", "rinv_done", "xn_done", "xT_done", "hT_done"))
        wxr_in, wyr_in, wq_in, wkv_in, wao_in, wlo_in = (
            sem(n) for n in ("wxr_in", "wyr_in", "wq_in", "wkv_in", "wao_in", "wlo_in"))
        ga_in, gl_in = [sem(f"ga_in{j}") for j in range(4)], [sem(f"gl_in{j}") for j in range(4)]
        wo_in = [sem(f"wo_in{j}") for j in range(2)]
        bd_zero, bd_in, sin_in, sin_done, clam_exp = (sem(n) for n in ("bd_zero", "bd_in", "sin_in", "sin_done", "clam_exp"))
        branch_mm, branch_out = sem("branch_mm"), sem("branch_out")
        conv_done, ix_done, expa_done, om_done, sqrt_done, lru_done = (
            sem(n) for n in ("conv_done", "ix_done", "expa_done", "om_done", "sqrt_done", "lru_done"))
        qkv_mm, rope_done, v_done, qkT_mm, qkT_done = (
            sem(n) for n in ("qkv_mm", "rope_done", "v_done", "qkT_mm", "qkT_done"))
        score_mm, score_read, negm_done, exp_done, prob_done = (
            sem(n) for n in ("score_mm", "score_read", "negm_done", "exp_done", "prob_done"))
        pT_mm, pT_done, pv_mm, oT_done = (sem(n) for n in ("pT_mm", "pT_done", "pv_mm", "oT_done"))
        gate_mm, sgate_done, merged_done = sem("gate_mm"), sem("sgate_done"), sem("merged_done")
        bias_in, bias_done, sel_done = sem("bias_in"), sem("bias_done"), sem("sel_done")
        wo_mm, x2_done, h2_done, h2T_mm, h2T_done, logit_mm, logit_done = (
            sem(n) for n in ("wo_mm", "x2_done", "h2_done", "h2T_mm", "h2T_done", "logit_mm", "logit_done"))
        xb_in, acc_out, h2_out = ([sem(f"{n}{q}") for q in range(2)] for n in ("xb_in", "acc_out", "h2_out"))
        gffn_in = sem("gffn_in")
        gexp_in, gexp_done, mask_done, rank_mm, iota_built, meta_const, table_done = (
            sem(n) for n in ("gexp_in", "gexp_done", "mask_done", "rank_mm", "iota_built", "meta_const", "table_done"))
        w_arrived = [sem(f"w_arrived{i}") for i in range(NU)]
        unit_mm = [sem(f"unit_mm{i}") for i in range(NU)]
        onehot_done, meta_mm, idx_done, cur_done, rows_in, rowsT_mm, rowsT_done = (
            sem(n) for n in ("onehot_done", "meta_mm", "idx_done", "cur_done", "rows_in", "rowsT_mm", "rowsT_done"))
        sel_ready, gclip_done, gsig_done, act_done, actT_mm, actT_done, y_done, added = (
            sem(n) for n in ("sel_ready", "gclip_done", "gsig_done", "act_done", "actT_mm", "actT_done", "y_done", "added"))
        acc_in = [sem(f"acc_in{t}") for t in range(NT)]
        fssq, frms, frinv, fin_done, stored = (sem(n) for n in ("fssq", "frms", "frinv", "fin_done", "stored"))
        dve_step, pool_step, reg_seen = sem("dve_step"), sem("pool_step"), sem("reg_seen")

        def wait_reg(eng, signal, value):
            eng.wait_ge(signal, value)
            eng.sem_inc(reg_seen)

        block = ctx.enter_context(nc.Block())
        N_CONST = 14
        N_BUILT = 11

        @block.sync
        def _(sp):
            for t in range(NT):
                sp.dma_start(xin[:, t, :], x_t[t]).then_inc(x_in[t], 16)
                if t == 3:
                    sp.dma_start(wxr_sb, w_in_v[:, :, OFF_XR:OFF_XR + LW]).then_inc(wxr_in, 16)
            sp.dma_start(wyr_sb, w_in_v[:, :, OFF_YR:OFF_YR + LW]).then_inc(wyr_in, 16)
            sp.dma_start(wq_sb, w_in_v[:, :, OFF_Q:OFF_Q + QW]).then_inc(wq_in, 16)
            sp.dma_start(wkv_sb, w_in_v[:, :, OFF_KV:OFF_KV + 2 * KVW]).then_inc(wkv_in, 16)
            sp.wait_ge(branch_mm, 8)
            wao_v = w_attn_o[0].rearrange("(g h d) n -> g d h n", g=N_KV, h=GROUP)
            for g in range(N_KV):
                sp.dma_start(wao_sb[64 * g:64 * g + 64], wao_v[g]).then_inc(wao_in, 16)
            sp.wait_ge(branch_mm, 16)
            sp.dma_start(wlo_sb, w_lru_o[0].rearrange("(k p) n -> p k n", p=P)).then_inc(wlo_in, 16)

            def gates(j):
                sp.dma_start(ga_sb[j], w_in_v[:, :, OFF_GA + 256 * j:OFF_GA + 256 * (j + 1)]).then_inc(ga_in[j], 16)
                sp.dma_start(gl_sb[j], w_in_v[:, :, OFF_GL + 256 * j:OFF_GL + 256 * (j + 1)]).then_inc(gl_in[j], 16)

            sp.wait_ge(branch_mm, 32)
            sp.wait_ge(qkv_mm, NT)
            sp.wait_ge(rope_done, NT)
            sp.wait_ge(score_read, N_KV)
            gates(0)
            gates(1)
            sp.wait_ge(gate_mm, 16)
            gates(2)
            sp.wait_ge(gate_mm, 32)
            gates(3)
            sp.wait_ge(gate_mm, 48)
            sp.dma_start(wo_sb[0], w_out_v[:, :, 0:HALF]).then_inc(wo_in[0], 16)
            sp.wait_ge(gate_mm, 64)
            sp.dma_start(wo_sb[1], w_out_v[:, :, HALF:D]).then_inc(wo_in[1], 16)

            def unit(i, e):
                col = (0, D, HALF, D + HALF, 0, HALF)[i]
                src = wgu_v if i < 4 else wdn_v
                s_ = src[:, e, :, col:col + HALF] if isinstance(e, int) else (
                    src[:, ds(e, 1), :, col:col + HALF].rearrange("p a k n -> p (a k) n"))
                sp.dma_start(wu[i], s_).then_inc(w_arrived[i], 16)

            for i in range(NU):
                unit(i, 0)
            sp.wait_ge(table_done, 1)
            with sp.Fori(1, NE) as e:
                end = sp.value_load(ends[0:1, ds(e - 1, 1)], min_val=1, max_val=MAXC)
                for i in range(NU):
                    wait_reg(sp, unit_mm[i], end)
                    wait_reg(sp, w_arrived[i], e * 16)
                    unit(i, e)
            total = sp.value_load(ends[0:1, NE - 1:NE], min_val=1, max_val=MAXC)
            wait_reg(sp, added, total * 16 + 16)
            wait_reg(sp, unit_mm[5], total)
            for t in range(NT):
                sp.dma_start(fin[t], acc_t[t]).then_inc(acc_in[t], 16)
            for t in range(NT):
                sp.wait_ge(fin_done, t + 1)
                sp.dma_start(out_t[t], fin[t]).then_inc(stored, 16)
            sp.wait_ge(stored, 16 * NT)

        @block.tensor
        def _(pe):
            mm = nc.tensor.matmul
            tr = nc.tensor.transpose
            pe.wait_ge(small_built, N_BUILT)
            for t in range(NT):
                pe.wait_ge(xn_done, t + 1)
                if t >= 2:
                    pe.wait_ge(hT_done, 2 * (t - 1))
                for k in range(KD):
                    last = tr(bank(2 * (t % 2), 2)[:, k * P:(k + 1) * P], xin[:, t, k * P:(k + 1) * P], ident[:])
                    if k % 4 == 3:
                        last.then_inc(xT_done, 1)
            pe.wait_ge(hT_done, 2 * NT)
            n = 0
            for w, arrived in ((wxr_sb, wxr_in), (wyr_sb, wyr_in)):
                pe.wait_ge(arrived, 16)
                for m in range(LM):
                    for th in range(2):
                        if n >= 4:
                            pe.wait_ge(branch_out, n - 3)
                        for k in range(KD):
                            last = mm(bank(4 + n % 4), w[:, k, m * P:(m + 1) * P], hT[:, k, th * HALF:(th + 1) * HALF],
                                      start=(k == 0), stop=(k == KD - 1))
                        last.then_inc(branch_mm, 1)
                        n += 1
            pe.wait_ge(bd_in, 64)
            for m in range(LM):
                pe.wait_ge(conv_done, m + 1)
                for g in range(2):
                    for th in range(2):
                        pe.wait_ge(branch_out, n - 3)
                        mm(bank(4 + n % 4), bd[:, g, m, :], xc[:, m, th * HALF:(th + 1) * HALF],
                           start=True, stop=True).then_inc(branch_mm, 1)
                        n += 1

            def project(b):
                if b >= 1:
                    pe.wait_ge(rope_done, b)
                    pe.wait_ge(v_done, b)
                if b >= 3:
                    pe.wait_ge(oT_done, 2 * (b - 2))
                for k in range(KD):
                    mm(bank(0), hT[:, k, b * P:(b + 1) * P], wq_sb[:, k, :].rearrange("p (g h d) -> p h g d", g=N_KV, h=GROUP), start=(k == 0), stop=(k == KD - 1))
                for k in range(KD):
                    last = mm(bank(1)[:, 0:2 * KVW], hT[:, k, b * P:(b + 1) * P], wkv_sb[:, k, :],
                              start=(k == 0), stop=(k == KD - 1))
                last.then_inc(qkv_mm, 1)

            def scores(b):
                pe.wait_ge(rope_done, b + 1)
                if b == 0:
                    pe.wait_ge(branch_out, 32)
                if b >= 2:
                    pe.wait_ge(pT_done, 2 * (b - 1))
                for h in range(GROUP):
                    tr(bank(6)[:, h * P:(h + 1) * P], qk[:, 2 * h:2 * h + 2, :], ident[:])
                tr(bank(7)[:, 0:P], qk[:, N_Q:N_Q + 2, :], ident[:]).then_inc(qkT_mm, 1)
                pe.wait_ge(qkT_done, 2 * (b + 1))
                if b >= 1:
                    pe.wait_ge(score_read, 2 * b)
                for g in range(N_KV):
                    for h in range(GROUP):
                        last = mm(bank(2 + 2 * g, 2)[:, h * 2 * P:(h + 1) * 2 * P], qT[64 * g:64 * g + 64, h, :],
                                  kT[64 * g:64 * g + 64, b * P:(b + 2) * P], start=True, stop=True)
                    last.then_inc(score_mm, 1)

            def values(b):
                for g in range(N_KV):
                    pe.wait_ge(prob_done, 2 * b + g + 1)
                    if g == 0 and b + 1 < NT:
                        pe.wait_ge(qkT_done, 2 * (b + 2))
                    if 2 * b + g >= 1:
                        pe.wait_ge(pT_done, 2 * b + g)
                    for kb in range(2):
                        for h in range(GROUP):
                            last = tr(bank(6 + kb)[:, h * P:(h + 1) * P], prob[g][:, h, kb * P:(kb + 1) * P], ident[:])
                    last.then_inc(pT_mm, 1)
                    pe.wait_ge(pT_done, 2 * b + g + 1)
                    if b + 2 < NT:
                        pe.wait_ge(rope_done, b + 3)
                        pe.wait_ge(v_done, b + 3)
                    if b >= 1:
                        pe.wait_ge(oT_done, 2 * (b - 1) + g + 1)
                    for kb in range(2):
                        last = mm(bank(g)[64 * g:64 * g + 64, :], vrow[:, (b + kb) % 4, 64 * g:64 * g + 64],
                                  pT[:, kb * HALF:(kb + 1) * HALF], start=(kb == 0), stop=(kb == 1))
                    last.then_inc(pv_mm, 1)

            pe.wait_ge(wq_in, 16)
            pe.wait_ge(wkv_in, 16)
            for s in range(NT + 2):
                if s < NT:
                    project(s)
                if 1 <= s <= NT:
                    scores(s - 1)
                if s >= 2:
                    values(s - 2)

            pe.wait_ge(wao_in, 32)
            pe.wait_ge(wlo_in, 16)
            pe.wait_ge(oT_done, 2 * NT)
            pe.wait_ge(lru_done, LM)
            for n in range(2 * KD):
                j, th = n // 2, n % 2
                b0 = 4 * (n % 2)
                if n % 4 == 0:
                    pe.wait_ge(ga_in[j // 2], 16)
                    pe.wait_ge(gl_in[j // 2], 16)
                if n == 1:
                    pe.wait_ge(pT_done, 2 * NT)
                if n >= 2:
                    pe.wait_ge(merged_done, n - 1)
                tok = slice(th * HALF, (th + 1) * HALF)
                c = (j % 2) * P
                for k in range(KD):
                    last = mm(bank(b0), ga_sb[j // 2][:, k, c:c + P], hT[:, k, tok], start=(k == 0), stop=(k == KD - 1))
                last.then_inc(gate_mm, 1)
                for k in range(KD):
                    last = mm(bank(b0 + 1), gl_sb[j // 2][:, k, c:c + P], hT[:, k, tok], start=(k == 0), stop=(k == KD - 1))
                last.then_inc(gate_mm, 1)
                for k in range(GROUP):
                    last = mm(bank(b0 + 2), wao_sb[:, k, j * P:(j + 1) * P], oT[:, k, tok], start=(k == 0), stop=(k == GROUP - 1))
                last.then_inc(gate_mm, 1)
                for k in range(LM):
                    last = mm(bank(b0 + 3), wlo_sb[:, k, j * P:(j + 1) * P], lruT[:, k, tok], start=(k == 0), stop=(k == LM - 1))
                last.then_inc(gate_mm, 1)

            pe.wait_ge(merged_done, 2 * KD)

            def router_T(t):
                pe.wait_ge(h2_done, t + 1)
                if t >= 1:
                    pe.wait_ge(h2T_done, t)
                for k in range(KD):
                    last = tr(bank(4, 2)[:, k * P:(k + 1) * P], h2[t % 2][:, k * P:(k + 1) * P], ident[:])
                last.then_inc(h2T_mm, 1)

            def router_mm(t):
                pe.wait_ge(h2T_done, t + 1)
                if t >= 2:
                    pe.wait_ge(logit_done, t - 1)
                for k in range(KD):
                    last = mm(bank(6 + t % 2)[:, 0:NE], h2T[:, k * P:(k + 1) * P], wrt[:, k, :],
                              start=(k == 0), stop=(k == KD - 1))
                last.then_inc(logit_mm, 1)

            for t in range(NT + 2):
                if t < NT:
                    if t >= 2:
                        pe.wait_ge(x2_done, t - 1)
                    for half in range(2):
                        if t == 0:
                            pe.wait_ge(wo_in[half], 16)
                        for k in range(KD):
                            last = mm(bank(2 * (t % 2) + half), merged[:, k, t * P:(t + 1) * P], wo_sb[half][:, k, :],
                                      start=(k == 0), stop=(k == KD - 1))
                    last.then_inc(wo_mm, 1)
                if t >= 2:
                    router_mm(t - 2)
                if 1 <= t <= NT:
                    router_T(t - 1)

            pe.wait_ge(mask_done, 1)
            for t in range(NT):
                for s in range(t + 1):
                    mm(bank(0)[:, t * NE:(t + 1) * NE], (tri_b if s == t else ones_b)[:], mask_b[:, s, :],
                       start=(s == 0), stop=(s == t))
            for s in range(NT):
                last = mm(bank(1)[:, 0:NE], ones_b[:], mask_b[:, s, :], start=(s == 0), stop=(s == NT - 1))
            last.then_inc(rank_mm, 1)

            pe.wait_ge(table_done, 1)

            def chunk_meta(e):
                for t in range(NT):
                    last = mm(bank(7)[:, 0:NMETA], onehot[:, t, :], meta[:, ds(e * (NT * NMETA) + t * NMETA, NMETA)],
                              start=(t == 0), stop=(t == NT - 1))
                last.then_inc(meta_mm, 1)

            def chunk_rowsT():
                for k in range(KD):
                    last = tr(bank(6, 2)[:, k * P:(k + 1) * P], rows_g[:, k * P:(k + 1) * P], ident[:])
                last.then_inc(rowsT_mm, 1)

            total = pe.value_load(ends[0:1, NE - 1:NE], min_val=1, max_val=MAXC)
            first_e = pe.value_load(chunk_e[0:1, 0:1], min_val=0, max_val=NE - 1)
            pe.wait_ge(onehot_done, 1)
            chunk_meta(first_e)
            pe.wait_ge(rows_in, 16)
            chunk_rowsT()
            pe.wait_ge(bias_done, 1)
            pe.wait_ge(sel_done, 4)
            with pe.Fori(0, MAXC) as j:
                with pe.If(j < total):
                    e = pe.value_load(chunk_e[0:1, ds(j, 1)], min_val=0, max_val=NE - 1)
                    e_next = pe.value_load(chunk_e[0:1, ds(j + 1, 1)], min_val=0, max_val=NE - 1)
                    tail = pe.value_load(chunk_tail[0:1, ds(j, 1)], min_val=0, max_val=1)
                    BIAS_COL = (0, D, HALF, D + HALF, 2 * D, 2 * D + HALF)

                    def full_unit(i, stat, k0, k1):
                        if k0 == 0:
                            pe.wait_ge(w_arrived[i], e * 16 + 16)
                            mm(bank(i), sel_cur[0:96, :], bias3[0:96, BIAS_COL[i]:BIAS_COL[i] + HALF], start=True, stop=False)
                        for k in range(k0, k1):
                            last = mm(bank(i), stat[:, k * P:(k + 1) * P], wu[i][:, k, :], start=False, stop=(k == KD - 1))
                        if k1 == KD:
                            last.then_inc(unit_mm[i], 1)

                    def tail_product(b_, units, stat_of, ks):
                        for k in ks:
                            for q in range(QUART):
                                i, c = units[q // 2], QC * (q % 2)
                                dst = bank(b_)[TAIL * q:TAIL * (q + 1), 0:QC]
                                if k == 0:
                                    if q % 2 == 0:
                                        pe.wait_ge(w_arrived[i], e * 16 + 16)
                                    mm(dst, sel_cur[0:96, 0:TAIL], bias3[0:96, BIAS_COL[i] + c:BIAS_COL[i] + c + QC],
                                       start=True, stop=False)
                                last = mm(dst, stat_of(k, q), wu[i][:, k, c:c + QC], start=False, stop=(k == KD - 1))
                                if k == KD - 1 and q % 2 == 1:
                                    last.then_inc(unit_mm[i], 1)

                    def next_meta():
                        pe.wait_ge(onehot_done, j + 2)
                        chunk_meta(e_next)

                    def next_rows():
                        pe.wait_ge(rows_in, j * 16 + 32)
                        chunk_rowsT()

                    pe.wait_ge(rowsT_done, j + 1)
                    pe.wait_ge(sel_ready, j + 1)
                    with pe.If(tail < 1):
                        full_unit(0, rowsT, 0, KD)
                        full_unit(1, rowsT, 0, KD)
                        next_meta()
                        full_unit(2, rowsT, 0, KD)
                        full_unit(3, rowsT, 0, KD)
                        next_rows()
                        for half in range(2):
                            pe.wait_ge(act_done, j * 2 + half + 2)
                            for k in range(4):
                                last = tr(bank(2 * half)[:, k * P:(k + 1) * P], uclip[:, half, k * P:(k + 1) * P], ident[:])
                            last.then_inc(actT_mm, 1)
                            pe.wait_ge(actT_done, j * 2 + half + 1)
                            if half == 0:
                                pe.wait_ge(y_done, j * 2 + 1)
                            for i in (4, 5):
                                full_unit(i, actT, 4 * half, 4 * half + 4)
                    with pe.If(tail > 0):
                        tail_product(0, (0, 2), lambda k, q: rowsT[:, k * P + TAIL * q:k * P + TAIL * (q + 1)], range(KD))
                        next_meta()
                        tail_product(1, (1, 3), lambda k, q: rowsT[:, k * P + TAIL * q:k * P + TAIL * (q + 1)], range(KD))
                        next_rows()
                        for half in range(2):
                            pe.wait_ge(act_done, j * 2 + half + 2)
                            tr(bank(2 * half)[:, 0:P], uclip[:, 0, half * P:(half + 1) * P], ident[:]).then_inc(actT_mm, 1)
                            pe.wait_ge(actT_done, j * 2 + half + 1)
                            if half == 0:
                                pe.wait_ge(y_done, j * 2 + 1)
                            tail_product(4, (4, 5), lambda k, q: actT[:, half * P + TAIL * (k // 2):half * P + TAIL * (k // 2 + 1)],
                                         range(half, KD, 2))

        @block.scalar
        def _(act):
            loads = [
                (gmix[:], norm_mix_g[0].rearrange("(k p) -> p k", p=P)),
                (pos_i[:], positions[0].rearrange("(t p) -> p t", p=P)),
                (freq[:], inv_freq[None, :].to_broadcast([P, HD // 2])),
                (convb[:], conv_b[0].rearrange("(m p) -> p m", p=P)),
                (brg[:], b_rg[0].rearrange("(m p) -> p m", p=P)),
                (big[:], b_ig[0].rearrange("(m p) -> p m", p=P)),
                (lam[:], lru_lambda[0].rearrange("(m p) -> p m", p=P)),
                (sink[:], attn_sinks[0][None, :].to_broadcast([P, N_Q])),
                (wrt[:], w_router[0].rearrange("(k p) e -> p k e", p=P)),
                (brt[:], b_router[0][None, :].to_broadcast([P, NE])),
            ] + [(convw[:, c, :], conv_w[0, c].rearrange("(m p) -> p m", p=P)) for c in range(CONV)]
            assert len(loads) == N_CONST
            with nc.allow_non_contiguous_dma("small vectors, one element per partition"):
                for dst, src in loads:
                    act.dma_start(dst, src).then_inc(consts_in, 16)
            act.wait_ge(small_built, N_BUILT)
            for t in range(NT):
                act.wait_ge(x_in[t], 16)
                act.activation(region_a[:, 0:D], xin[:, t, :], ACT.Square, accum_out=ssq[:, 0, t:t + 1]).then_inc(ssq_done, 1)
                act.wait_ge(ssq_done, t + 1)
                act.activation(rms[:, 0, t:t + 1], ssq[:, 0, t:t + 1], ACT.Sqrt, bias=eps[:], scale=1.0 / D).then_inc(rms_done, 1)
            act.wait_ge(sin_in, 1)
            act.activation(sin, sin, ACT.Sin).then_inc(sin_done, 1)
            act.activation(cos, cos, ACT.Sin).then_inc(sin_done, 1)
            act.wait_ge(clam_exp, 1)
            act.activation(clam[:, 1, :], clam[:, 0, :], ACT.Exp, scale=-1.0).then_inc(clam_exp, 1)
            for n in range(16):
                m, th = (n // 2) % LM, n % 2
                act.wait_ge(branch_mm, n + 1)
                if n < 8:
                    act.activation(xr[:, m, 3 + th * HALF:3 + (th + 1) * HALF], bank(4 + n % 4), ACT.Copy).then_inc(branch_out, 1)
                else:
                    act.activation(lruT[:, m, th * HALF:(th + 1) * HALF], bank(4 + n % 4), ACT.Gelu_apprx_tanh).then_inc(branch_out, 1)
            for n in range(16, 32):
                m, g, th = (n - 16) // 4, (n // 2) % 2, n % 2
                act.wait_ge(branch_mm, n + 1)
                dst = xr[:, m, 3 + th * HALF:3 + (th + 1) * HALF] if g == 0 else igate[:, m, th * HALF:(th + 1) * HALF]
                act.activation(dst, bank(4 + n % 4), ACT.Sigmoid, bias=(brg, big)[g][:, m:m + 1]).then_inc(branch_out, 1)
            act.wait_ge(branch_out, 32)
            for m in range(LM):
                act.wait_ge(ix_done, m + 1)
                act.activation(xc[:, m, :], xr[:, m, 3:3 + SEQ], ACT.Exp, scale=clam[:, 5, m:m + 1]).then_inc(expa_done, 1)
                act.wait_ge(expa_done, 2 * m + 1)
                act.activation(xr[:, m, 3:3 + SEQ], xr[:, m, 3:3 + SEQ], ACT.Tanh, scale=clam[:, 5, m:m + 1]).then_inc(expa_done, 1)
            for m in range(LM):
                act.wait_ge(om_done, m + 1)
                act.activation(xr[:, m, 3:3 + SEQ], xr[:, m, 3:3 + SEQ], ACT.Sqrt, scale=-1.0).then_inc(sqrt_done, 1)
            for s in range(NT + 2):
                if 1 <= s <= NT:
                    b = s - 1
                    act.wait_ge(qkT_mm, b + 1)
                    if b >= 1:
                        act.wait_ge(score_mm, 2 * b)
                    act.activation(qT, bank(6), ACT.Copy).then_inc(qkT_done, 1)
                    act.activation(kT[:, (b + 1) * P:(b + 2) * P], bank(7)[:, 0:P], ACT.Copy).then_inc(qkT_done, 1)
                if s >= 2:
                    b = s - 2
                    for g in range(N_KV):
                        act.wait_ge(pT_mm, 2 * b + g + 1)
                        if 2 * b + g >= 1:
                            act.wait_ge(pv_mm, 2 * b + g)
                        act.activation(pT, bank(6, 2), ACT.Copy).then_inc(pT_done, 1)
                        act.wait_ge(pv_mm, 2 * b + g + 1)
                        act.activation(oT[64 * g:64 * g + 64, :, b * P:(b + 1) * P],
                                       bank(g)[64 * g:64 * g + 64, :].rearrange("p (h q) -> p h q", h=GROUP),
                                       ACT.Copy).then_inc(oT_done, 1)
                if 1 <= s <= NT:
                    b = s - 1
                    for g in range(N_KV):
                        act.wait_ge(negm_done, 2 * b + g + 1)
                        for h in range(GROUP):
                            gh = GROUP * g + h
                            act.activation(prob[g][:, h, :], prob[g][:, h, :], ACT.Exp, bias=negm[:, gh:gh + 1],
                                           accum_out=sume[:, gh:gh + 1])
                        act.activation(esink[:, GROUP * g:GROUP * (g + 1)], esink[:, GROUP * g:GROUP * (g + 1)],
                                       ACT.Exp).then_inc(exp_done, 1)
            for n in range(2 * KD):
                if n >= 2:
                    act.wait_ge(merged_done, n - 1)
                for q in range(2):
                    act.wait_ge(gate_mm, 4 * n + q + 1)
                    act.activation(sgate[n % 2][q], bank(4 * (n % 2) + q), ACT.Sigmoid).then_inc(sgate_done, 1)
            def h2T_out(t):
                act.wait_ge(h2T_mm, t + 1)
                if t >= 1:
                    act.wait_ge(logit_mm, t)
                act.activation(h2T, bank(4, 2), ACT.Copy).then_inc(h2T_done, 1)

            for t in range(NT):
                act.wait_ge(x2_done, t + 1)
                if t >= 2:
                    act.wait_ge(h2T_mm, t - 1)
                    act.wait_ge(h2_out[t % 2], 16 * (t // 2))
                act.activation(h2[t % 2], xb[t % 2], ACT.Square, accum_out=ssq[:, 1, t:t + 1]).then_inc(ssq_done, 1)
                act.wait_ge(ssq_done, NT + t + 1)
                act.activation(rms[:, 1, t:t + 1], ssq[:, 1, t:t + 1], ACT.Sqrt, bias=eps[:], scale=1.0 / D).then_inc(rms_done, 1)
                if t >= 1:
                    h2T_out(t - 1)
            h2T_out(NT - 1)
            act.wait_ge(gexp_in, 1)
            act.activation(gate4, gate4, ACT.Exp).then_inc(gexp_done, 1)

            act.wait_ge(table_done, 1)
            total = act.value_load(ends[0:1, NE - 1:NE], min_val=1, max_val=MAXC)

            def rowsT_out():
                act.activation(rowsT, bank(6, 2), ACT.Copy).then_inc(rowsT_done, 1)

            act.sem_inc(y_done)
            act.wait_ge(rowsT_mm, 1)
            rowsT_out()
            with act.Fori(0, MAXC) as j:
                with act.If(j < total):
                    tail = act.value_load(chunk_tail[0:1, ds(j, 1)], min_val=0, max_val=1)

                    def sigmoids(part):
                        for half in range(2):
                            act.wait_ge(gclip_done, j * 2 + half + 1)
                            act.activation(part(gsig, half), part(gclip, half), ACT.Sigmoid, scale=ALPHA).then_inc(gsig_done, 1)
                        act.wait_ge(rowsT_mm, j + 2)
                        rowsT_out()

                    def outputs(width, banks, last_unit):
                        for half in range(2):
                            act.wait_ge(actT_mm, j * 2 + half + 1)
                            act.activation(actT[:, half * width:(half + 1) * width], bank(2 * half)[:, 0:width],
                                           ACT.Copy).then_inc(actT_done, 1)
                        wait_reg(act, cur_done, j + 1)
                        wait_reg(act, added, j * 16 + 16)
                        for half in range(2):
                            act.wait_ge(unit_mm[last_unit[half]], j + 1)
                            act.activation(yrow[:, half * width:(half + 1) * width], banks[half], ACT.Copy,
                                           scale=w_cur[:, 0:1]).then_inc(y_done, 1)

                    with act.If(tail < 1):
                        sigmoids(lambda ap, half: ap[:, half, :])
                        outputs(HALF, (bank(4), bank(5)), (4, 5))
                    with act.If(tail > 0):
                        sigmoids(lambda ap, half: ap[:, 0, half * P:(half + 1) * P])
                        outputs(P, (bank(4)[:, 0:P], bank(4)[:, P:2 * P]), (5, 5))
            for t in range(NT):
                act.wait_ge(acc_in[t], 16)
                act.activation(fjunk, fin[t], ACT.Square, accum_out=ssq[:, 2, t:t + 1]).then_inc(fssq, 1)
                act.wait_ge(fssq, t + 1)
                act.activation(rms[:, 2, t:t + 1], ssq[:, 2, t:t + 1], ACT.Sqrt, bias=eps[:], scale=1.0 / D).then_inc(frms, 1)

        @block.gpsimd
        def _(pool):
            g = nc.gpsimd
            steps = [0]

            def then(ins):
                steps[0] += 1
                ins.then_inc(pool_step, 1)
                pool.wait_ge(pool_step, steps[0])

            then(g.memset(ident[:], 0.0))
            g.affine_select(out=ident[:], in_=ident[:], compare_op=ALU.not_equal, fill=1.0, base=0,
                            pattern=[[-1, P]], channel_multiplier=1).then_inc(small_built, 1)
            g.memset(eps[:], EPS).then_inc(small_built, 1)
            then(g.memset(bd, 0.0))
            with nc.allow_non_contiguous_dma("64-wide diagonal blocks"):
                for q, w in enumerate((w_rg, w_ig)):
                    wv = w[0].rearrange("(m h) i j -> h i m j", h=2)
                    for h in range(2):
                        g.dma_start(bd[64 * h:64 * h + 64, q, :, 64 * h:64 * h + 64], wv[h]).then_inc(bd_in, 16)
            for m_ in (mask[:], mask_first):
                then(g.memset(m_, 0.0))
                then(g.affine_select(out=m_, in_=m_, compare_op=ALU.is_ge, fill=NEG_INF, base=P,
                                     pattern=[[-1, 2 * P]], channel_multiplier=1))
                ins = g.affine_select(out=m_, in_=m_, compare_op=ALU.is_ge, fill=NEG_INF, base=-1,
                                      pattern=[[1, 2 * P]], channel_multiplier=-1)
                if m_ is mask_first:
                    then(ins)
                else:
                    ins.then_inc(small_built, 1)
            g.affine_select(out=mask_first, in_=mask_first, compare_op=ALU.is_ge, fill=NEG_INF, base=-P,
                            pattern=[[1, 2 * P]], channel_multiplier=0).then_inc(small_built, 1)
            g.memset(ones_b[:], 1.0).then_inc(small_built, 1)
            then(g.memset(tri_b[:], 1.0))
            g.affine_select(out=tri_b[:], in_=tri_b[:], compare_op=ALU.is_ge, fill=0.0, base=-1,
                            pattern=[[1, P]], channel_multiplier=-1).then_inc(small_built, 1)
            for dst, pattern, mult in ((iota_e, [[1, NE]], 0), (iota_j, [[1, MAXC + 1]], 0), (iota_p, [[0, 1]], 1),
                                       (iota_t, [[P, NT]], 0)):
                g.iota(dst[:], pattern=pattern, base=0, channel_multiplier=mult,
                       allow_small_or_imprecise_dtypes=True).then_inc(small_built, 1)
            g.memset(row_next[:], 0).then_inc(small_built, 1)
            for q in range(QUART):
                then(g.memset(quart[TAIL * q:TAIL * (q + 1), :], float(q)))
            for m in range(LM):
                pool.wait_ge(branch_out, 16 + 4 * (m + 1))
                g.tensor_tensor(out=igate[:, m, :], in0=igate[:, m, :], in1=xc[:, m, :], op=ALU.mult).then_inc(ix_done, 1)
            pool.wait_ge(lru_done, LM)
            pool.wait_ge(oT_done, 2 * NT)
            pool.wait_ge(pT_mm, 2 * NT)
            for q in range(3):
                g.dma_start(bstage[32 * q:32 * q + 32, 0:2 * D], b_gate_up[0]).then_inc(bias_in, 16)
                g.dma_start(bstage[32 * q:32 * q + 32, 2 * D:3 * D], b_down[0]).then_inc(bias_in, 16)
            g.memset(sel[0:96, :], 0.0).then_inc(sel_done, 1)
            pool.wait_ge(sel_done, 1)
            for q in range(3):
                v = sel[32 * q:32 * q + 32, :].rearrange("p (e m) -> p e m", e=NE)
                g.affine_select(out=v, in_=v, compare_op=ALU.not_equal, fill=1.0, base=0,
                                pattern=[[-1, NE], [0, P]], channel_multiplier=1).then_inc(sel_done, 1)
                pool.wait_ge(sel_done, q + 2)
            pool.wait_ge(merged_done, 2 * KD)
            pool.wait_ge(bias_done, 1)
            g.dma_start(gffn, norm_ffn_g[0][None, :].to_broadcast([P, D])).then_inc(gffn_in, 16)
            for t in range(2):
                g.dma_start(xb[t], x_t[t]).then_inc(xb_in[t], 16)
            for t in range(NT):
                pool.wait_ge(x2_done, t + 1)
                g.dma_start(acc_t[t], xb[t % 2]).then_inc(acc_out[t % 2], 16)
                pool.wait_ge(h2_done, t + 1)
                g.dma_start(h2_t[t], h2[t % 2]).then_inc(h2_out[t % 2], 16)
                if t + 2 < NT:
                    pool.wait_ge(acc_out[t % 2], 16 * (t // 2 + 1))
                    g.dma_start(xb[t % 2], x_t[t + 2]).then_inc(xb_in[t % 2], 16)
            for q in range(2):
                pool.wait_ge(acc_out[q], 16 * (NT // 2))
                pool.wait_ge(h2_out[q], 16 * (NT // 2))
            pool.wait_ge(logit_mm, NT)
            g.iota(iota_s, pattern=[[1, SEQ]], base=0, channel_multiplier=0,
                   allow_small_or_imprecise_dtypes=True).then_inc(iota_built, 1)
            g.dma_start(gfin, norm_final_g[None, :].to_broadcast([P, D])).then_inc(added, 16)

            def gather():
                g.indirect_dma_start(out=rows_g, out_offset=None, in_=h2_rows,
                                     in_offset=bass.IndirectOffsetOnAxis(ap=row_next[:, 0:1], axis=0),
                                     bounds_check=SEQ - 1, oob_is_err=False).then_inc(rows_in, 16)

            def add(dst, col, width, rows):
                g.indirect_dma_start(out=dst, out_offset=bass.IndirectOffsetOnAxis(ap=row_cur[:, col:col + 1], axis=0),
                                     in_=yrow[:, 0:width], in_offset=None, bounds_check=rows - 1, oob_is_err=False,
                                     compute_op=ALU.add).then_inc(added, 16)

            pool.wait_ge(table_done, 1)
            total = pool.value_load(ends[0:1, NE - 1:NE], min_val=1, max_val=MAXC)
            pool.wait_ge(idx_done, 1)
            gather()
            with pool.Fori(0, MAXC) as j:
                with pool.If(j < total):
                    wait_reg(pool, idx_done, j + 2)
                    wait_reg(pool, rowsT_mm, j + 1)
                    gather()
                    wait_reg(pool, y_done, j * 2 + 3)
                    wait_reg(pool, cur_done, j + 1)
                    tail = pool.value_load(chunk_tail[0:1, ds(j, 1)], min_val=0, max_val=1)
                    with pool.If(tail < 1):
                        add(acc_rows, 0, D, SEQ)
                    with pool.If(tail > 0):
                        add(acc_rows.rearrange("t (q c) -> (t q) c", q=QUART), 1, QC, SEQ * QUART)

        @block.vector
        def _(dve):
            v = nc.vector
            steps = [0]

            def then(ins):
                steps[0] += 1
                ins.then_inc(dve_step, 1)
                dve.wait_ge(dve_step, steps[0])

            def bc(ap, shape):
                return ap.to_broadcast(shape)

            dve.wait_ge(consts_in, 16 * N_CONST)
            dve.wait_ge(small_built, N_BUILT)

            def xnorm(t):
                dve.wait_ge(rms_done, t + 1)
                v.reciprocal(rinv[:, 0, t:t + 1], rms[:, 0, t:t + 1]).then_inc(rinv_done, 1)
                dve.wait_ge(rinv_done, t + 1)
                v.tensor_scalar(xin[:, t, :], xin[:, t, :], rinv[:, 0, t:t + 1], None, ALU.mult).then_inc(xn_done, 1)

            def hT_out(t):
                for q in range(2):
                    dve.wait_ge(xT_done, 2 * t + q + 1)
                    v.tensor_tensor(out=hT[:, 4 * q:4 * q + 4, t * P:(t + 1) * P],
                                    in0=bank(2 * (t % 2) + q).rearrange("p (k n) -> p k n", k=4),
                                    in1=bc(gmix[:, 4 * q:4 * q + 4, None], [P, 4, P]), op=ALU.mult).then_inc(hT_done, 1)

            for t in range(NT + 1):
                if t < NT:
                    xnorm(t)
                if t >= 1:
                    hT_out(t - 1)
            then(v.tensor_copy(pos_f[:], pos_i[:]))
            ang, turn = unit_view(region_a[:, 0:NT * 32], NT), unit_view(region_a[:, NT * 32:2 * NT * 32], NT)
            dve.wait_ge(ssq_done, NT)
            then(v.tensor_tensor(out=ang, in0=bc(pos_f[:, :, None], [P, NT, 32]), in1=bc(freq[:, None, :], [P, NT, 32]), op=ALU.mult))
            for dst, quarter in ((sin, 0.0), (cos, 0.25)):
                then(v.tensor_scalar(turn, ang, 1.0 / (2 * 3.141592653589793), quarter, ALU.mult, ALU.add))
                then(v.tensor_scalar(turn, turn, MAGIC, None, ALU.add))
                then(v.tensor_scalar(turn, turn, MAGIC, None, ALU.subtract))
                src = ang
                for c in TWO_PI_PARTS:
                    then(v.scalar_tensor_tensor(out=dst, in0=turn, scalar=-c, in1=src, op0=ALU.mult, op1=ALU.add))
                    src = dst
                pi = 3.1415925
                then(v.tensor_scalar(dst, dst, quarter * 2 * 3.141592653589793, pi, ALU.add, ALU.min))
                ins = v.tensor_scalar(dst, dst, -pi, None, ALU.max)
                if quarter:
                    ins.then_inc(sin_in, 1)
                else:
                    then(ins)
            then(v.tensor_scalar(clam[:, 2, :], lam[:], -1.0, None, ALU.mult))
            v.tensor_tensor(out=clam[:, 0, :], in0=lam[:], in1=clam[:, 2, :], op=ALU.max).then_inc(clam_exp, 1)
            dve.wait_ge(clam_exp, 2)
            then(v.tensor_scalar(clam[:, 3, :], clam[:, 1, :], 2.0, None, ALU.add))
            then(v.reciprocal(clam[:, 4, :], clam[:, 3, :]))
            then(v.tensor_tensor(out=clam[:, 1, :], in0=clam[:, 1, :], in1=clam[:, 4, :], op=ALU.mult))
            then(v.tensor_tensor(out=clam[:, 3, :], in0=clam[:, 1, :], in1=clam[:, 1, :], op=ALU.mult))
            then(v.memset(clam[:, 4, :], 0.0))
            for q in range(9, 0, -1):
                then(v.scalar_tensor_tensor(out=clam[:, 4, :], in0=clam[:, 4, :], scalar=1.0 / (2 * q + 1), in1=clam[:, 3, :],
                                            op0=ALU.add, op1=ALU.mult))
            then(v.scalar_tensor_tensor(out=clam[:, 4, :], in0=clam[:, 4, :], scalar=1.0, in1=clam[:, 1, :], op0=ALU.add, op1=ALU.mult))
            then(v.tensor_scalar(clam[:, 2, :], clam[:, 2, :], 0.0, -LRU_C, ALU.max, ALU.mult))
            then(v.scalar_tensor_tensor(out=clam[:, 5, :], in0=clam[:, 4, :], scalar=-2.0 * LRU_C, in1=clam[:, 2, :],
                                        op0=ALU.mult, op1=ALU.add))
            v.memset(kT[:, 0:P], 0.0)
            v.memset(vrow[:, 0, :], 0.0)
            dve.wait_ge(xT_done, 2 * NT)
            then(v.memset(xr[:, :, 0:3], 0.0))
            for m in range(LM):
                dve.wait_ge(branch_out, 2 * (m + 1))
                then(v.tensor_scalar(xc[:, m, :], xr[:, m, 3:3 + SEQ], convw[:, 3, m:m + 1], convb[:, m:m + 1], ALU.mult, ALU.add))
                for c in (2, 1, 0):
                    ins = v.scalar_tensor_tensor(out=xc[:, m, :], in0=xr[:, m, c:c + SEQ], scalar=convw[:, c, m:m + 1],
                                                 in1=xc[:, m, :], op0=ALU.mult, op1=ALU.add)
                    if c:
                        then(ins)
                    else:
                        ins.then_inc(conv_done, 1)
            a2 = region_a[:, A_COLS - SEQ:A_COLS]
            for m in range(LM):
                dve.wait_ge(expa_done, 2 * (m + 1))
                if m >= 1:
                    dve.wait_ge(om_done, m)
                then(v.tensor_tensor(out=a2, in0=xc[:, m, :], in1=xc[:, m, :], op=ALU.mult))
                v.scalar_tensor_tensor(out=xr[:, m, 3:3 + SEQ], in0=a2, scalar=1.0, in1=xr[:, m, 3:3 + SEQ],
                                       op0=ALU.add, op1=ALU.mult).then_inc(om_done, 1)

            def recur(m):
                dve.wait_ge(sqrt_done, m + 1)
                then(v.tensor_tensor(out=xr[:, m, 3:3 + SEQ], in0=xr[:, m, 3:3 + SEQ], in1=igate[:, m, :], op=ALU.mult))
                then(v.tensor_tensor_scan(igate[:, m, :], xc[:, m, :], xr[:, m, 3:3 + SEQ], 0.0, ALU.mult, ALU.add))
                v.tensor_tensor(out=lruT[:, m, :], in0=lruT[:, m, :], in1=igate[:, m, :], op=ALU.mult).then_inc(lru_done, 1)

            dve.wait_ge(sin_done, 2)
            for s in range(NT + 1):
                if s < NT:
                    dve.wait_ge(qkv_mm, s + 1)
                    if s >= 1:
                        dve.wait_ge(qkT_mm, s)
                        dve.wait_ge(rope_done, s)
                    nh = N_Q + N_KV
                    src = psum[:, 0:nh * HD].rearrange("p (h d) -> p h d", d=HD)
                    t1, t2 = src[:, :, 0:32], src[:, :, 32:64]
                    c_, s_ = bc(cos[:, s:s + 1, :], [P, nh, 32]), bc(sin[:, s:s + 1, :], [P, nh, 32])
                    v.tensor_tensor(out=ropa, in0=t1, in1=c_, op=ALU.mult)
                    then(v.tensor_tensor(out=ropb, in0=t2, in1=s_, op=ALU.mult))
                    then(v.tensor_tensor(out=qk[:, :, 0:32], in0=ropa, in1=ropb, op=ALU.subtract))
                    v.tensor_tensor(out=ropa, in0=t2, in1=c_, op=ALU.mult)
                    then(v.tensor_tensor(out=ropb, in0=t1, in1=s_, op=ALU.mult))
                    v.tensor_tensor(out=qk[:, :, 32:64], in0=ropa, in1=ropb, op=ALU.add).then_inc(rope_done, 1)
                    v.tensor_copy(vrow[:, (s + 1) % 4, :], bank(1)[:, KVW:2 * KVW]).then_inc(v_done, 1)
                if s < LM:
                    recur(s)
                if s >= 1:
                    b = s - 1
                    for g in range(N_KV):
                        hs = slice(GROUP * g, GROUP * (g + 1))
                        dve.wait_ge(score_mm, 2 * b + g + 1)
                        if b >= 1:
                            dve.wait_ge(pT_mm, 2 * (b - 1) + g + 1)
                        v.scalar_tensor_tensor(out=prob[g], in0=bank(2 + 2 * g, 2).rearrange("p (h k) -> p h k", h=GROUP),
                                               scalar=HD ** -0.5, in1=bc((mask[:] if b else mask_first)[:, None, :], [P, GROUP, 2 * P]),
                                               op0=ALU.mult, op1=ALU.add).then_inc(score_read, 1)
                        dve.wait_ge(score_read, 2 * b + g + 1)
                        then(v.tensor_reduce(out=mx[:, hs], in_=prob[g], axis=AX, op=ALU.max))
                        then(v.tensor_tensor(out=mx[:, hs], in0=mx[:, hs], in1=sink[:, hs], op=ALU.max))
                        then(v.tensor_scalar(negm[:, hs], mx[:, hs], -1.0, None, ALU.mult))
                        v.tensor_tensor(out=esink[:, hs], in0=sink[:, hs], in1=negm[:, hs], op=ALU.add).then_inc(negm_done, 1)
                    for g in range(N_KV):
                        hs = slice(GROUP * g, GROUP * (g + 1))
                        dve.wait_ge(exp_done, 2 * b + g + 1)
                        then(v.tensor_tensor(out=rden[:, hs], in0=sume[:, hs], in1=esink[:, hs], op=ALU.add))
                        then(v.reciprocal(rden[:, hs], rden[:, hs]))
                        v.tensor_tensor(out=prob[g], in0=prob[g], in1=bc(rden[:, hs, None], [P, GROUP, 2 * P]),
                                        op=ALU.mult).then_inc(prob_done, 1)
            for n in range(2 * KD):
                b0, tok = 4 * (n % 2), slice((n % 2) * HALF, (n % 2 + 1) * HALF)
                dve.wait_ge(gate_mm, 4 * n + 3)
                dve.wait_ge(sgate_done, 2 * n + 1)
                if n == 0:
                    dve.wait_ge(pT_mm, 2 * NT)
                    dve.wait_ge(pv_mm, 2 * NT)
                if n >= 1:
                    dve.wait_ge(merged_done, n)
                v.tensor_tensor(out=part_a, in0=sgate[n % 2][0], in1=bank(b0 + 2), op=ALU.mult)
                dve.wait_ge(gate_mm, 4 * n + 4)
                dve.wait_ge(sgate_done, 2 * n + 2)
                then(v.tensor_tensor(out=part_b, in0=sgate[n % 2][1], in1=bank(b0 + 3), op=ALU.mult))
                v.tensor_tensor(out=merged[:, n // 2, tok], in0=part_a, in1=part_b, op=ALU.add).then_inc(merged_done, 1)
                if n == 8:
                    dve.wait_ge(bias_in, 96)
                    then(v.tensor_copy(bias3[0:96, :], bstage[0:96, :]))
                if n == 9:
                    then(v.tensor_tensor(out=bstage[0:96, :], in0=bstage[0:96, :], in1=bias3[0:96, :], op=ALU.subtract))
                if n == 10:
                    v.tensor_copy(bias3[32:64, :], bstage[32:64, :])
                    then(v.tensor_copy(bias3[64:96, :], bstage[64:96, :]))
                if n == 11:
                    then(v.tensor_tensor(out=bstage[64:96, :], in0=bstage[64:96, :], in1=bias3[64:96, :], op=ALU.subtract))
                    v.tensor_copy(bias3[64:96, :], bstage[64:96, :]).then_inc(bias_done, 1)
            def top(t):
                dve.wait_ge(logit_mm, t + 1)
                v.tensor_tensor(out=logit[:, t, :], in0=bank(6 + t % 2)[:, 0:NE], in1=brt[:], op=ALU.add).then_inc(logit_done, 1)
                dve.wait_ge(logit_done, t + 1)
                then(v.max(top_v[:, t, :], logit[:, t, :]))
                then(v.max_index(top_i[:, t, :], top_v[:, t, :], logit[:, t, :]))

            dve.wait_ge(gffn_in, 16)
            for t in range(NT):
                dve.wait_ge(wo_mm, t + 1)
                dve.wait_ge(xb_in[t % 2], 16 * (t // 2 + 1))
                v.tensor_tensor(out=xb[t % 2], in0=bank(2 * (t % 2), 2), in1=xb[t % 2], op=ALU.add).then_inc(x2_done, 1)
                dve.wait_ge(rms_done, NT + t + 1)
                v.reciprocal(rinv[:, 1, t:t + 1], rms[:, 1, t:t + 1]).then_inc(rinv_done, 1)
                dve.wait_ge(rinv_done, NT + t + 1)
                v.scalar_tensor_tensor(out=h2[t % 2], in0=xb[t % 2], scalar=rinv[:, 1, t:t + 1], in1=gffn,
                                       op0=ALU.mult, op1=ALU.mult).then_inc(h2_done, 1)
                if t >= 2:
                    top(t - 2)
            top(NT - 2)
            top(NT - 1)
            v.tensor_copy(top_f, top_i)
            v.tensor_tensor(out=gate4, in0=top_v[:, :, 0:TOPK], in1=bc(top_v[:, :, 0:1], [P, NT, TOPK]),
                            op=ALU.subtract).then_inc(gexp_in, 1)
            dve.wait_ge(gexp_done, 1)
            then(v.tensor_reduce(out=gsum, in_=gate4, axis=AX, op=ALU.add))
            then(v.reciprocal(gsum, gsum))
            then(v.tensor_tensor(out=gate4, in0=gate4, in1=bc(gsum[:, :, None], [P, NT, TOPK]), op=ALU.mult))
            dve.wait_ge(iota_built, 1)
            for k in range(TOPK):
                then(v.tensor_tensor(out=oh, in0=bc(iota_e[:, None, :], [P, NT, NE]), in1=bc(top_f[:, :, k:k + 1], [P, NT, NE]), op=ALU.is_equal))
                dst = gate_d if k == 0 else ohg
                then(v.tensor_tensor(out=dst, in0=oh, in1=bc(gate4[:, :, k:k + 1], [P, NT, NE]), op=ALU.mult))
                if k == 0:
                    then(v.tensor_copy(mask_d, oh))
                else:
                    v.tensor_tensor(out=mask_d, in0=mask_d, in1=oh, op=ALU.add)
                    then(v.tensor_tensor(out=gate_d, in0=gate_d, in1=ohg, op=ALU.add))
            v.tensor_copy(mask_b, mask_d).then_inc(mask_done, 1)
            mv = meta.rearrange("p (e t c) -> p t e c", e=NE, t=NT)
            v.tensor_copy(mv[:, :, :, 0], bc(iota_t[:, :, None], [P, NT, NE]))
            v.tensor_copy(mv[:, :, :, 1], bc(iota_p[:, :, None], [P, NT, NE]))
            v.memset(mv[:, :, :, 2], -float(FAR))
            then(v.tensor_copy(mv[:, :, :, 3], gate_d))
            then(v.tensor_tensor(out=gate_r, in0=gate_d, in1=mv[:, :, :, 3], op=ALU.subtract))
            then(v.tensor_copy(mv[:, :, :, 4], gate_r))
            then(v.tensor_tensor(out=gate_r, in0=gate_r, in1=mv[:, :, :, 4], op=ALU.subtract))
            then(v.tensor_copy(mv[:, :, :, 5], gate_r))
            dve.wait_ge(rank_mm, 1)
            then(v.scalar_tensor_tensor(out=oh, in0=bank(0)[:, 0:NT * NE].rearrange("p (t e) -> p t e", t=NT), scalar=1.0,
                                        in1=mask_d, op0=ALU.add, op1=ALU.mult))
            then(v.tensor_scalar(rank.rearrange("p e t -> p t e"), oh, -1.0, None, ALU.add))
            then(v.tensor_copy(cnt, bank(1)[:, 0:NE]))
            then(v.memset(nch, 1.0))
            for q in range(1, SEQ // P):
                then(v.scalar_tensor_tensor(out=nch, in0=cnt, scalar=float(P * q), in1=nch, op0=ALU.is_gt, op1=ALU.add))
            then(v.memset(cexc, 0.0))
            then(v.tensor_tensor_scan(cinc, nch, cexc, 0.0, ALU.add, ALU.add))
            then(v.tensor_tensor(out=cexc, in0=cinc, in1=nch, op=ALU.subtract))
            nj = MAXC + 1
            jb = bc(iota_j[:, :, None], [P, nj, NE])
            then(v.tensor_tensor(out=tcmp, in0=bc(cinc[:, None, :], [P, nj, NE]), in1=jb, op=ALU.is_le))
            then(v.tensor_reduce(out=tab_f[:, 0, :], in_=tcmp, axis=AX, op=ALU.add))
            then(v.tensor_scalar(tab_f[:, 0, :], tab_f[:, 0, :], float(NE - 1), None, ALU.min))
            then(v.tensor_copy(chunk_e[:], tab_f[:, 0, :]))
            then(v.tensor_tensor(out=tcmp, in0=bc(cexc[:, None, :], [P, nj, NE]), in1=jb, op=ALU.is_le))
            then(v.tensor_tensor(out=tcmp2, in0=tcmp, in1=bc(cexc[:, None, :], [P, nj, NE]), op=ALU.mult))
            then(v.tensor_reduce(out=tab_f[:, 1, :], in_=tcmp2, axis=AX, op=ALU.max))
            then(v.tensor_tensor(out=tab_f[:, 1, :], in0=iota_j[:], in1=tab_f[:, 1, :], op=ALU.subtract))
            then(v.tensor_scalar(tab_f[:, 1, :], tab_f[:, 1, :], float(NT - 1), None, ALU.min))
            then(v.tensor_copy(chunk_c[:], tab_f[:, 1, :]))
            then(v.tensor_tensor(out=tcmp2, in0=bc(cinc[:, None, :], [P, nj, NE]), in1=jb, op=ALU.is_le))
            then(v.tensor_tensor(out=tcmp, in0=tcmp, in1=tcmp2, op=ALU.subtract))
            then(v.tensor_tensor(out=tcmp, in0=tcmp, in1=bc(cnt[:, None, :], [P, nj, NE]), op=ALU.mult))
            then(v.tensor_reduce(out=tab_f[:, 2, :], in_=tcmp, axis=AX, op=ALU.add))
            then(v.scalar_tensor_tensor(out=tab_f[:, 2, :], in0=tab_f[:, 1, :], scalar=-float(P), in1=tab_f[:, 2, :],
                                        op0=ALU.mult, op1=ALU.add))
            then(v.tensor_scalar(tab_f[:, 2, :], tab_f[:, 2, :], float(TAIL), None, ALU.is_le))
            then(v.scalar_tensor_tensor(out=tab_f[:, 2, :], in0=tab_f[:, 1, :], scalar=1.0, in1=tab_f[:, 2, :],
                                        op0=ALU.is_ge, op1=ALU.mult))
            then(v.tensor_copy(chunk_tail[:], tab_f[:, 2, :]))
            v.tensor_copy(ends[:], cinc).then_inc(table_done, 1)

            dve.wait_ge(table_done, 1)
            total = dve.value_load(ends[0:1, NE - 1:NE], min_val=1, max_val=MAXC)

            def slots(e, c, tail):
                of_e = rank[:, ds(e, 1), :].rearrange("p a t -> p (a t)")
                with dve.If(tail < 1):
                    v.tensor_tensor(out=onehot, in0=iota_s[:, ds(c * P, P)][:, None, :].to_broadcast([P, NT, P]),
                                    in1=of_e[:, :, None].to_broadcast([P, NT, P]), op=ALU.is_equal).then_inc(onehot_done, 1)
                with dve.If(tail > 0):
                    for q in range(QUART):
                        ins = v.tensor_tensor(out=onehot[:, :, TAIL * q:TAIL * (q + 1)],
                                              in0=iota_s[:, ds(c * P, TAIL)][:, None, :].to_broadcast([P, NT, TAIL]),
                                              in1=of_e[:, :, None].to_broadcast([P, NT, TAIL]), op=ALU.is_equal)
                    ins.then_inc(onehot_done, 1)

            def selector(e):
                v.tensor_copy(sel_cur[0:96, :], sel[0:96, ds(e * P, P)]).then_inc(sel_ready, 1)

            N_STEP = 5

            def rows_of(base):
                v.tensor_copy(meta_s[:], bank(7)[:, 0:NMETA]).then_inc(dve_step, 1)
                dve.wait_ge(dve_step, base + 1)
                v.tensor_tensor(out=row_f[:, 0:1], in0=meta_s[:, 0:1], in1=meta_s[:, 1:2], op=ALU.add).then_inc(dve_step, 1)
                v.tensor_tensor(out=w_next[:, 1:2], in0=meta_s[:, 3:4], in1=meta_s[:, 4:5], op=ALU.add).then_inc(dve_step, 1)
                dve.wait_ge(dve_step, base + 3)
                v.tensor_tensor(out=w_next[:, 0:1], in0=w_next[:, 1:2], in1=meta_s[:, 5:6], op=ALU.add)
                v.scalar_tensor_tensor(out=row_f[:, 1:2], in0=meta_s[:, 2:3], scalar=float(FAR), in1=row_f[:, 0:1],
                                       op0=ALU.add, op1=ALU.add).then_inc(dve_step, 1)
                dve.wait_ge(dve_step, base + 4)
                v.scalar_tensor_tensor(out=row_f[:, 2:3], in0=row_f[:, 1:2], scalar=float(QUART), in1=quart[:],
                                       op0=ALU.mult, op1=ALU.add).then_inc(dve_step, 1)
                dve.wait_ge(dve_step, base + 5)
                v.tensor_copy(row_next[:], row_f[:]).then_inc(idx_done, 1)

            e0 = dve.value_load(chunk_e[0:1, 0:1], min_val=0, max_val=NE - 1)
            c0 = dve.value_load(chunk_c[0:1, 0:1], min_val=0, max_val=NT - 1)
            t0 = dve.value_load(chunk_tail[0:1, 0:1], min_val=0, max_val=1)
            dve.sem_inc(act_done)
            dve.wait_ge(sel_done, 4)
            selector(e0)
            slots(e0, c0, t0)
            dve.wait_ge(meta_mm, 1)
            base0 = steps[0]
            rows_of(base0)
            base0 += N_STEP
            PER = N_STEP + 4
            with dve.Fori(0, MAXC) as j:
                with dve.If(j < total):
                    e_next = dve.value_load(chunk_e[0:1, ds(j + 1, 1)], min_val=0, max_val=NE - 1)
                    c_next = dve.value_load(chunk_c[0:1, ds(j + 1, 1)], min_val=0, max_val=NT - 1)
                    t_next = dve.value_load(chunk_tail[0:1, ds(j + 1, 1)], min_val=0, max_val=1)
                    tail = dve.value_load(chunk_tail[0:1, ds(j, 1)], min_val=0, max_val=1)
                    here = j * PER + base0
                    wait_reg(dve, meta_mm, j + 1)
                    slots(e_next, c_next, t_next)
                    wait_reg(dve, idx_done, j + 1)
                    wait_reg(dve, act_done, j * 2 + 1)

                    def gate_clip(part, half, b_, signal):
                        dve.wait_ge(signal, j + 1)
                        v.tensor_scalar(part(gclip, half), b_, LIMIT, None, ALU.min).then_inc(gclip_done, 1)

                    def swiglu(part, half, b_, signal, step):
                        dve.wait_ge(signal, j + 1)
                        v.tensor_scalar(part(uclip, half), b_, LIMIT, -LIMIT, ALU.min, ALU.max).then_inc(dve_step, 1)
                        dve.wait_ge(gsig_done, j * 2 + half + 1)
                        v.tensor_tensor(out=part(gclip, half), in0=part(gclip, half), in1=part(gsig, half),
                                        op=ALU.mult).then_inc(dve_step, 1)
                        dve.wait_ge(dve_step, step + 2)
                        v.scalar_tensor_tensor(out=part(uclip, half), in0=part(uclip, half), scalar=1.0, in1=part(gclip, half),
                                               op0=ALU.add, op1=ALU.mult).then_inc(act_done, 1)

                    def next_rows(step):
                        wait_reg(dve, y_done, j * 2 + 1)
                        wait_reg(dve, added, j * 16 + 16)
                        v.tensor_copy(w_cur[:], w_next[:, 0:1])
                        v.tensor_copy(row_cur[:], row_next[:, 1:3]).then_inc(cur_done, 1)
                        wait_reg(dve, meta_mm, j + 2)
                        wait_reg(dve, rows_in, j * 16 + 16)
                        wait_reg(dve, cur_done, j + 1)
                        rows_of(step)

                    with dve.If(tail < 1):
                        def part(ap, half):
                            return ap[:, half, :]

                        gate_clip(part, 0, bank(0), unit_mm[0])
                        swiglu(part, 0, bank(1), unit_mm[1], here)
                        next_rows(here + 2)
                        gate_clip(part, 1, bank(2), unit_mm[2])
                        swiglu(part, 1, bank(3), unit_mm[3], here + 2 + N_STEP)
                    with dve.If(tail > 0):
                        def part(ap, half):
                            return ap[:, 0, half * P:(half + 1) * P]

                        gate_clip(part, 0, bank(0)[:, 0:P], unit_mm[2])
                        gate_clip(part, 1, bank(0)[:, P:2 * P], unit_mm[2])
                        next_rows(here)
                        swiglu(part, 0, bank(1)[:, 0:P], unit_mm[3], here + N_STEP)
                        swiglu(part, 1, bank(1)[:, P:2 * P], unit_mm[3], here + N_STEP + 2)
                    wait_reg(dve, actT_mm, j * 2 + 2)
                    selector(e_next)
            for t in range(NT):
                dve.wait_ge(frms, t + 1)
                v.reciprocal(rinv[:, 2, t:t + 1], rms[:, 2, t:t + 1]).then_inc(frinv, 1)
                dve.wait_ge(frinv, t + 1)
                v.scalar_tensor_tensor(out=fin[t], in0=fin[t], scalar=rinv[:, 2, t:t + 1], in1=gfin,
                                       op0=ALU.mult, op1=ALU.mult).then_inc(fin_done, 1)


_INS = ["x", "positions", "norm_mix_g", "w_in", "conv_w", "conv_b", "w_rg", "b_rg", "w_ig", "b_ig", "lru_lambda",
        "attn_sinks", "w_attn_o", "w_lru_o", "w_out", "norm_ffn_g", "w_router", "b_router", "w_gate_up", "b_gate_up",
        "w_down", "b_down", "norm_final_g"]


def kernel(**inputs):
    import numpy as _np
    import concourse.bacc as _bacc
    from concourse import mybir as _mybir
    from concourse.bass_utils import run_bass_kernel_spmd as _run

    nc = _bacc.Bacc("TRN2", target_bir_lowering=False, num_devices=1)
    arrays, args = {}, []
    for name in _INS:
        a = _np.ascontiguousarray(inputs[name])
        arrays[f"in_{name}_dram"] = a
        args.append(nc.dram_tensor(f"in_{name}_dram", a.shape, _mybir.dt.from_np(a.dtype), kind="ExternalInput").ap())
    half = HD // 2
    freq = (_np.float32(1.0) / (_np.float32(10000.0) ** (_np.arange(0, HD, 2, dtype=_np.float32) / _np.float32(HD)))).astype(_np.float32)
    assert freq.shape == (half,)
    arrays["in_inv_freq_dram"] = freq
    args.append(nc.dram_tensor("in_inv_freq_dram", freq.shape, _mybir.dt.float32, kind="ExternalInput").ap())
    args.append(nc.dram_tensor("out_0_dram", (1, SEQ, D), _mybir.dt.float32, kind="ExternalOutput").ap())
    hybrid_decoder_block(nc, *args)
    r = _run(nc, [arrays], core_ids=[0])
    return r.results[0]["out_0_dram"]
```

```python
import concourse.bass as bass
from concourse import mybir
from contextlib import ExitStack

SEQ, D = 1024, 1024
P = 128
NT = SEQ // P
KD = D // P
HALF = 512
N_Q, N_KV, HD = 8, 2, 64
GROUP = N_Q // N_KV
QW, KVW, LW = N_Q * HD, N_KV * HD, D // 2
LM = LW // P
CONV = 4
NE, TOPK = 32, 4
MAXC = SEQ * TOPK // P + NE
NJ = MAXC + 2
NU = 6
SLOTS = 8
TAIL = 32
QUART = P // TAIL
QC = D // QUART
UNIT = KD * HALF
SHIFT = 4
SUBS = 24
NBUF = 4
ACT_T = (12, 18)
ON_POOL = (5, 9, 13, 17, 20)
FAR = 4096
NEG_INF = -1e30
LRU_C = 8.0
LIMIT, ALPHA = 7.0, 1.702
EPS = 1e-6
NMETA = 6
A_COLS = 6528
TWO_PI_PARTS = (6.28125, 0.00193500518798828125, 3.0199159819562e-07)
MAGIC = 12582912.0


def hybrid_decoder_block(nc, x, positions, norm_mix_g, w_in, conv_w, conv_b, w_rg, b_rg, w_ig, b_ig,
                         lru_lambda, attn_sinks, w_attn_o, w_lru_o, w_out, norm_ffn_g, w_router, b_router,
                         w_gate_up, b_gate_up, w_down, b_down, norm_final_g, inv_freq, out):
    f32, bf16, i32, u32 = mybir.dt.float32, mybir.dt.bfloat16, mybir.dt.int32, mybir.dt.uint32
    ALU, ACT = mybir.AluOpType, mybir.ActivationFunctionType
    AX = mybir.AxisListType.X
    ds = bass.ds

    h2_rows = nc.dram_tensor("h2_rows", [SEQ, D], f32, kind="Internal").ap()
    acc_rows = nc.dram_tensor("acc_rows", [SEQ, D], f32, kind="Internal").ap()

    x_t = x[0].rearrange("(t p) d -> t p d", p=P)
    out_t = out[0].rearrange("(t p) d -> t p d", p=P)
    h2_t = h2_rows.rearrange("(t p) d -> t p d", p=P)
    acc_t = acc_rows.rearrange("(t p) d -> t p d", p=P)
    w_in_v = w_in[0].rearrange("(k p) n -> p k n", p=P)
    OFF_Q, OFF_KV, OFF_XR = 0, QW, QW + 2 * KVW
    OFF_YR, OFF_GA = OFF_XR + LW, OFF_XR + 2 * LW
    OFF_GL = OFF_GA + D
    w_out_v = w_out[0].rearrange("(k p) n -> p k n", p=P)
    wgu_v = w_gate_up[0].rearrange("e (k p) n -> p e k n", p=P)
    wdn_v = w_down[0].rearrange("e (k p) n -> p e k n", p=P)

    ctx = ExitStack()
    with ctx:
        def sb(name, shape, dt=f32):
            return ctx.enter_context(nc.sbuf_tensor(name, shape, dt))

        def sem(name):
            return ctx.enter_context(nc.semaphore(name))

        f32r = mybir.dt.float32r

        def sub_unit(n):
            if n < 16:
                return n // 4, 2 * (n % 4)
            return 4 + (n - 16) // 2 % 2, 4 * ((n - 16) // 4) + 2 * (n % 2)

        def next_base():
            return -(-nc.sbuf_base // 32) * 32

        at_ring = next_base()
        ring = sb("ring", [P, SLOTS * UNIT])
        at_m = next_base()
        region_m = sb("region_m", [P, LM * (SEQ + 3) + LM * SEQ])
        at_s = next_base()
        region_s = sb("region_s", [P, LM * SEQ])
        at_a = next_base()
        region_a = sb("region_a", [P, A_COLS])

        def over(name, shape, base, col):
            return nc.alloc_sbuf_tensor_at(name, shape, f32r, offset=base + 4 * col)

        w_hi = over("w_hi", [P, NBUF, 2 * HALF], at_ring, 2 * UNIT)
        w_lo = over("w_lo", [P, NBUF, 2 * HALF], at_ring, 3 * UNIT)
        rows_hi, rows_lo = over("rows_hi", [P, D], at_m, 5632), over("rows_lo", [P, D], at_m, 5632 + D)
        act_hi, act_lo = over("act_hi", [P, D], at_a, A_COLS - 2 * D), over("act_lo", [P, D], at_a, A_COLS - D)

        def half_slot(n, count=1):
            return ring[:, n * UNIT // 2:(n + count) * UNIT // 2]

        def unit_view(ap, k):
            return ap.rearrange("p (k n) -> p k n", k=k)

        hT = unit_view(ring[:, 4 * UNIT:6 * UNIT], KD)
        oT = unit_view(ring[:, 6 * UNIT:7 * UNIT], GROUP)
        lruT = unit_view(ring[:, 7 * UNIT:8 * UNIT], LM)
        wxr_sb, wyr_sb = unit_view(half_slot(0, 2), KD), unit_view(half_slot(2, 2), KD)
        wq_sb, wkv_sb = unit_view(half_slot(4, 2), KD), unit_view(half_slot(6), KD)
        wao_sb, wlo_sb = unit_view(half_slot(0, 2), GROUP), unit_view(half_slot(2, 2), LM)
        ga_sb = [unit_view(half_slot(h), KD) for h in (7, 4, 7, 4)]
        gl_sb = [unit_view(half_slot(h), KD) for h in (6, 5, 6, 5)]
        wo_sb = [unit_view(half_slot(6, 2), KD), unit_view(half_slot(4, 2), KD)]
        bd = half_slot(7)[:, 0:2 * LM * P].rearrange("p (g m n) -> p g m n", g=2, m=LM)

        mask_first = half_slot(7)[:, 1024:1024 + 2 * P]
        cos = half_slot(7)[:, 1280:1280 + NT * 32].rearrange("p (t d) -> p t d", t=NT)
        sin = half_slot(7)[:, 1536:1536 + NT * 32].rearrange("p (t d) -> p t d", t=NT)

        xin = unit_view(region_m[:, 0:NT * D], NT)
        xr = unit_view(region_m[:, 0:LM * (SEQ + 3)], LM)
        xc = unit_view(region_m[:, LM * (SEQ + 3):LM * (SEQ + 3) + LM * SEQ], LM)
        merged = unit_view(region_m[:, 0:KD * SEQ], KD)
        rows_g = [region_m[:, 0:D], region_m[:, 2 * D:3 * D]]
        yrow = [region_m[:, D:2 * D], region_a[:, 2 * D:3 * D]]
        uclip = unit_view(region_m[:, 3 * D:4 * D], 2)
        gclip, gsig = region_m[:, 4 * D:4 * D + HALF], region_m[:, 4 * D + HALF:5 * D]
        rowsT_tail = region_m[:, 5120:5120 + KD * TAIL]
        actT_tail = region_m[:, 5376:5376 + 2 * P]
        sel_cur = region_m[:, 7680:7680 + P].bitcast(bf16).rearrange("p (u s) -> p u s", u=2)

        igate = unit_view(region_s[:, :], LM)
        bias3 = region_s[:, 0:1536].bitcast(bf16)
        place = [ring[:, (i + SHIFT) % SLOTS * UNIT:((i + SHIFT) % SLOTS + 1) * UNIT] for i in range(NU)]
        wu = [unit_view(p_, KD) for p_ in place]
        onehot = region_s[:, 1536:2048].bitcast(bf16).rearrange("p (t s) -> p t s", t=NT)
        sel = region_s[:, 2048:4096].bitcast(bf16)

        at = [0]

        def take(n):
            at[0] += n
            assert at[0] <= A_COLS, at[0]
            return region_a[:, at[0] - n:at[0]]

        qk = take((N_Q + N_KV) * HD).rearrange("p (h d) -> p h d", d=HD)
        ropa = take((N_Q + N_KV) * HD // 2).rearrange("p (h d) -> p h d", d=HD // 2)
        ropb = take((N_Q + N_KV) * HD // 2).rearrange("p (h d) -> p h d", d=HD // 2)
        qT = take(GROUP * P).rearrange("p (h q) -> p h q", h=GROUP)
        kT = take((NT + 1) * P)
        vrow = take(4 * P).rearrange("p (b d) -> p b d", b=4)
        prob = [take(GROUP * 2 * P).rearrange("p (h k) -> p h k", h=GROUP) for _ in range(N_KV)]
        pT = take(2 * GROUP * P)
        at[0] = 0
        sgate = [[take(HALF) for _ in range(2)] for _ in range(2)]
        part_a, part_b = take(HALF), take(HALF)
        piece_at = ((at_s, 1536), (at_a, at[0]))
        take(2 * (SEQ + 2 * P))
        h_hi, h_lo, g_hi, g_lo = [], [], [], []
        for q, (base, col) in enumerate(piece_at):
            for tiles, name, width in ((h_hi, "h_hi", SEQ), (h_lo, "h_lo", SEQ), (g_hi, "g_hi", 2 * P), (g_lo, "g_lo", 2 * P)):
                tiles.append(over(f"{name}{q}", [P, width], base, col))
                col += width
        bstage = region_m[:, 5 * SEQ:5 * SEQ + 3 * D]
        wo_hi = [over(f"wo_hi{q}", [P, UNIT], at_ring, (4 + 2 * q) * UNIT) for q in range(2)]
        wo_lo = [over(f"wo_lo{q}", [P, UNIT], at_ring, (5 + 2 * q) * UNIT) for q in range(2)]
        m_hi = [over(f"m_hi{q}", [P, KD, P], at_s, 1536 + q * D) for q in range(2)]
        m_lo = over("m_lo", [P, KD, SEQ], at_m, 0)
        at[0] = 0
        xb = [take(D), take(D)]
        h2 = [take(D), take(D)]
        h2T, gffn = take(D), take(D)
        logit = take(NT * NE).rearrange("p (t e) -> p t e", t=NT)
        top_v = take(NT * 8).rearrange("p (t k) -> p t k", t=NT)
        top_i = take(NT * 8).bitcast(u32).rearrange("p (t k) -> p t k", t=NT)
        at[0] = 0
        iota_s = take(SEQ)
        rank = take(NE * NT).rearrange("p (e t) -> p e t", e=NE)
        meta = take(NE * NT * NMETA // 2).bitcast(bf16)
        oh = take(NE * NT).rearrange("p (t e) -> p t e", t=NT)
        ohg = take(NE * NT).rearrange("p (t e) -> p t e", t=NT)
        mask_d = take(NE * NT).rearrange("p (t e) -> p t e", t=NT)
        gate_d = take(NE * NT).rearrange("p (t e) -> p t e", t=NT)
        gate_r = take(NE * NT).rearrange("p (t e) -> p t e", t=NT)
        mask_b = take(NE * NT // 2).bitcast(bf16).rearrange("p (t e) -> p t e", t=NT)
        gfin = take(D)
        top_f = take(NT * 8).rearrange("p (t k) -> p t k", t=NT)
        gate4 = take(NT * TOPK).rearrange("p (t k) -> p t k", t=NT)
        gsum = take(NT)
        cnt, nch, cinc, cexc = (take(NE) for _ in range(4))
        tab_f = take(6 * NJ)[0:1].rearrange("p (q j) -> p q j", q=6)
        ended, begun, oh_c, tab_c = take(NE), take(NE), take(NE), take(3)
        assert at[0] <= 6 * D
        fin = [ring[:, t * D:(t + 1) * D] for t in range(NT)]
        fjunk = ring[:, NT * D:(NT + 1) * D]

        ident = sb("ident", [P, P])
        mask = sb("mask", [P, 2 * P])
        wrt = sb("wrt", [P, KD, NE])
        ones_b, tri_b = sb("ones_b", [P, P], bf16), sb("tri_b", [P, P], bf16)
        iota_e = sb("iota_e", [P, NE])
        one_column = sb("one_column", [P, 3])
        iota_p, eps, quart = (one_column[:, n:n + 1] for n in range(3))
        iota_t = sb("iota_t", [P, NT])
        brt = sb("brt", [P, NE])
        gmix = sb("gmix", [P, KD])
        pos_i, pos_f = sb("pos_i", [P, NT], i32), sb("pos_f", [P, NT])
        freq = sb("freq", [P, HD // 2])
        convw, convb = sb("convw", [P, CONV, LM]), sb("convb", [P, LM])
        brg, big, lam = sb("brg", [P, LM]), sb("big", [P, LM]), sb("lam", [P, LM])
        clam = sb("clam", [P, 6, LM])
        sink = sb("sink", [P, N_Q])
        ssq, rms, rinv = sb("ssq", [P, 3, NT]), sb("rms", [P, 3, NT]), sb("rinv", [P, 3, NT])
        mx, negm, sume, esink, rden = (sb(n, [P, N_Q]) for n in ("mx", "negm", "sume", "esink", "rden"))
        slot_table, step_table = sb("slot_table", [P, NJ], i32), sb("step_table", [P, NJ], i32)
        ends = sb("ends", [P, NE], i32)
        meta_s = sb("meta_s", [P, NMETA])
        row_f, w_next, w_cur = sb("row_f", [P, 3]), sb("w_next", [P, 2, 2]), sb("w_cur", [P, 2])
        row_next, row_cur = sb("row_next", [P, 2, 3], i32), sb("row_cur", [P, 2, 2], i32)
        psum = ctx.enter_context(nc.psum_tensor("psum", [P, 8 * HALF], f32))

        def bank(n, count=1):
            return psum[:, n * HALF:(n + count) * HALF]

        x_in = [sem(f"x_in{t}") for t in range(NT)]
        gmix_in, consts_in, small_built = sem("gmix_in"), sem("consts_in"), sem("small_built")
        ident_built, eps_built = sem("ident_built"), sem("eps_built")
        ssq_done, rms_done, rinv_done, xn_done, xT_done, hT_done = (
            sem(n) for n in ("ssq_done", "rms_done", "rinv_done", "xn_done", "xT_done", "hT_done"))
        wxr_in, wyr_in, wq_in, wkv_in, wao_in, wlo_in = (
            sem(n) for n in ("wxr_in", "wyr_in", "wq_in", "wkv_in", "wao_in", "wlo_in"))
        ga_in, gl_in = [sem(f"ga_in{j}") for j in range(4)], [sem(f"gl_in{j}") for j in range(4)]
        wo_in = [sem(f"wo_in{j}") for j in range(2)]
        bd_zero, bd_in, sin_in, sin_done, clam_exp = (sem(n) for n in ("bd_zero", "bd_in", "sin_in", "sin_done", "clam_exp"))
        branch_mm, branch_out = sem("branch_mm"), sem("branch_out")
        conv_done, ix_done, expa_done, om_done, sqrt_done, lru_done = (
            sem(n) for n in ("conv_done", "ix_done", "expa_done", "om_done", "sqrt_done", "lru_done"))
        qkv_mm, rope_done, v_done, qkT_mm, qkT_done = (
            sem(n) for n in ("qkv_mm", "rope_done", "v_done", "qkT_mm", "qkT_done"))
        score_mm, score_read, negm_done, exp_done, prob_done = (
            sem(n) for n in ("score_mm", "score_read", "negm_done", "exp_done", "prob_done"))
        pT_mm, pT_done, pv_mm, oT_done = (sem(n) for n in ("pT_mm", "pT_done", "pv_mm", "oT_done"))
        gate_mm, proj_mm, sgate_done, merged_done = (sem(n) for n in ("gate_mm", "proj_mm", "sgate_done", "merged_done"))
        gate_hi, gate_lo = sem("gate_hi"), sem("gate_lo")
        wo_hi_done, wo_lo_done, m_hi_done, m_lo_done = (sem(n) for n in ("wo_hi_done", "wo_lo_done", "m_hi_done", "m_lo_done"))
        columns_done, columns_mm = sem("columns_done"), sem("columns_mm")
        bias_in, bias_done, sel_done = sem("bias_in"), sem("bias_done"), sem("sel_done")
        wo_mm, x2_done, h2_done, h2T_mm, h2T_done, logit_mm, logit_done = (
            sem(n) for n in ("wo_mm", "x2_done", "h2_done", "h2T_mm", "h2T_done", "logit_mm", "logit_done"))
        xb_in, acc_out, h2_out = ([sem(f"{n}{q}") for q in range(2)] for n in ("xb_in", "acc_out", "h2_out"))
        gffn_in = sem("gffn_in")
        gexp_in, gexp_done, mask_done, rank_mm, iota_built, meta_const, table_done = (
            sem(n) for n in ("gexp_in", "gexp_done", "mask_done", "rank_mm", "iota_built", "meta_const", "table_done"))
        w_arrived = [sem(f"w_arrived{i}") for i in range(NU)]
        unit_mm = [sem(f"unit_mm{i}") for i in range(NU)]
        onehot_done, meta_mm, idx_done, cur_done, rowsT_mm, rowsT_done = (
            sem(n) for n in ("onehot_done", "meta_mm", "idx_done", "cur_done", "rowsT_mm", "rowsT_done"))
        rows_in = [sem(f"rows_in{u}") for u in range(2)]
        hi_done, lo_dve, lo_pool, sub_mm, rows_lo_done, act_lo_done = (
            sem(n) for n in ("hi_done", "lo_dve", "lo_pool", "sub_mm", "rows_lo_done", "act_lo_done"))
        sel_ready, gclip_done, gsig_done, act_done, actT_mm, actT_done, y_done, added = (
            sem(n) for n in ("sel_ready", "gclip_done", "gsig_done", "act_done", "actT_mm", "actT_done", "y_done", "added"))
        acc_in = [sem(f"acc_in{t}") for t in range(NT)]
        fssq, frms, frinv, fin_done, stored = (sem(n) for n in ("fssq", "frms", "frinv", "fin_done", "stored"))
        dve_step, pool_step, reg_seen = sem("dve_step"), sem("pool_step"), sem("reg_seen")

        def load_slots(eng, j):
            w = eng.value_load(slot_table[0:1, ds(j, 1)], min_val=0, max_val=511)
            return w & 31, (w >> 5) & 7, (w >> 8) & 1

        def load_step(eng, j):
            w = eng.value_load(step_table[0:1, ds(j, 1)], min_val=0, max_val=(1 << 19) - 1)
            f = (w >> 6) & 63
            return w & 31, (w >> 5) & 1, f, (w >> 12) & 31, (w >> 17) & 1, f + ((w >> 18) & 1)

        def wait_reg(eng, signal, value):
            eng.wait_ge(signal, value)
            eng.sem_inc(reg_seen)

        block = ctx.enter_context(nc.Block())
        N_CONST = 13
        N_BUILT = 8

        @block.sync
        def _(sp):
            for t in range(NT):
                sp.dma_start(xin[:, t, :], x_t[t]).then_inc(x_in[t], 16)
            sp.dma_start(wxr_sb, w_in_v[:, :, OFF_XR:OFF_XR + LW]).then_inc(wxr_in, 16)
            sp.dma_start(wyr_sb, w_in_v[:, :, OFF_YR:OFF_YR + LW]).then_inc(wyr_in, 16)
            sp.dma_start(wq_sb, w_in_v[:, :, OFF_Q:OFF_Q + QW]).then_inc(wq_in, 16)
            sp.dma_start(wkv_sb, w_in_v[:, :, OFF_KV:OFF_KV + 2 * KVW]).then_inc(wkv_in, 16)
            sp.wait_ge(branch_mm, 8)
            wao_v = w_attn_o[0].rearrange("(g h d) n -> g d h n", g=N_KV, h=GROUP)
            for g in range(N_KV):
                sp.dma_start(wao_sb[64 * g:64 * g + 64], wao_v[g]).then_inc(wao_in, 16)
            sp.wait_ge(branch_mm, 16)
            sp.dma_start(wlo_sb, w_lru_o[0].rearrange("(k p) n -> p k n", p=P)).then_inc(wlo_in, 16)

            def gates(j):
                sp.dma_start(ga_sb[j], w_in_v[:, :, OFF_GA + 256 * j:OFF_GA + 256 * (j + 1)]).then_inc(ga_in[j], 16)
                sp.dma_start(gl_sb[j], w_in_v[:, :, OFF_GL + 256 * j:OFF_GL + 256 * (j + 1)]).then_inc(gl_in[j], 16)

            sp.wait_ge(branch_mm, 32)
            sp.wait_ge(qkv_mm, NT)
            sp.wait_ge(rope_done, NT)
            sp.wait_ge(score_read, N_KV)
            gates(0)
            gates(1)
            sp.wait_ge(gate_mm, 16)
            gates(2)
            sp.wait_ge(gate_mm, 32)
            gates(3)
            sp.wait_ge(gate_mm, 48)
            sp.dma_start(wo_sb[0], w_out_v[:, :, 0:HALF]).then_inc(wo_in[0], 16)
            sp.wait_ge(gate_mm, 64)
            sp.dma_start(wo_sb[1], w_out_v[:, :, HALF:D]).then_inc(wo_in[1], 16)
            sp.wait_ge(proj_mm, 4 * KD)

            def unit(i, e):
                col = (0, D, HALF, D + HALF, 0, HALF)[i]
                src = wgu_v if i < 4 else wdn_v
                s_ = src[:, e, :, col:col + HALF] if isinstance(e, int) else (
                    src[:, ds(e, 1), :, col:col + HALF].rearrange("p a k n -> p (a k) n"))
                sp.dma_start(wu[i], s_).then_inc(w_arrived[i], 16)

            sp.wait_ge(xb_in[0], 16)
            sp.wait_ge(xb_in[1], 16)
            sp.wait_ge(gffn_in, 16)
            unit(4, 0)
            unit(5, 0)
            sp.wait_ge(wo_mm, NT)
            for q in range(2):
                sp.wait_ge(acc_out[q], 16 * (NT // 2))
                sp.wait_ge(h2_out[q], 16 * (NT // 2))
            for i in range(4):
                unit(i, 0)
            sp.wait_ge(table_done, 1)
            with sp.Fori(1, NE) as e:
                end = sp.value_load(ends[0:1, ds(e - 1, 1)], min_val=1, max_val=MAXC)
                for i in range(NU):
                    wait_reg(sp, unit_mm[i], end)
                    wait_reg(sp, w_arrived[i], e * 16)
                    unit(i, e)
            total = sp.value_load(ends[0:1, NE - 1:NE], min_val=1, max_val=MAXC)
            wait_reg(sp, added, total * 16 + 32)
            wait_reg(sp, unit_mm[5], total)
            for t in range(NT):
                sp.dma_start(fin[t], acc_t[t]).then_inc(acc_in[t], 16)
            for t in range(NT):
                sp.wait_ge(fin_done, t + 1)
                sp.dma_start(out_t[t], fin[t]).then_inc(stored, 16)
            sp.wait_ge(stored, 16 * NT)

        @block.tensor
        def _(pe):
            mm = nc.tensor.matmul
            tr = nc.tensor.transpose
            pe.wait_ge(ident_built, 1)
            for t in range(NT):
                pe.wait_ge(xn_done, t + 1)
                if t >= 2:
                    pe.wait_ge(hT_done, 2 * (t - 1))
                for k in range(KD):
                    last = tr(bank(2 * (t % 2), 2)[:, k * P:(k + 1) * P], xin[:, t, k * P:(k + 1) * P], ident[:])
                    if k % 4 == 3:
                        last.then_inc(xT_done, 1)
            pe.wait_ge(hT_done, 2 * NT)
            n = 0
            for w, arrived in ((wxr_sb, wxr_in), (wyr_sb, wyr_in)):
                pe.wait_ge(arrived, 16)
                for m in range(LM):
                    for th in range(2):
                        if n >= 4:
                            pe.wait_ge(branch_out, n - 3)
                        for k in range(KD):
                            last = mm(bank(4 + n % 4), w[:, k, m * P:(m + 1) * P], hT[:, k, th * HALF:(th + 1) * HALF],
                                      start=(k == 0), stop=(k == KD - 1))
                        last.then_inc(branch_mm, 1)
                        n += 1
            pe.wait_ge(bd_in, 64)
            for m in range(LM):
                pe.wait_ge(conv_done, m + 1)
                for g in range(2):
                    for th in range(2):
                        pe.wait_ge(branch_out, n - 3)
                        mm(bank(4 + n % 4), bd[:, g, m, :], xc[:, m, th * HALF:(th + 1) * HALF],
                           start=True, stop=True).then_inc(branch_mm, 1)
                        n += 1

            def project(b):
                if b >= 1:
                    pe.wait_ge(rope_done, b)
                    pe.wait_ge(v_done, b)
                if b >= 3:
                    pe.wait_ge(oT_done, 2 * (b - 2))
                for k in range(KD):
                    mm(bank(0), hT[:, k, b * P:(b + 1) * P], wq_sb[:, k, :].rearrange("p (g h d) -> p h g d", g=N_KV, h=GROUP), start=(k == 0), stop=(k == KD - 1))
                for k in range(KD):
                    last = mm(bank(1)[:, 0:2 * KVW], hT[:, k, b * P:(b + 1) * P], wkv_sb[:, k, :],
                              start=(k == 0), stop=(k == KD - 1))
                last.then_inc(qkv_mm, 1)

            def turn_qk(b):
                pe.wait_ge(rope_done, b + 1)
                if b == 0:
                    pe.wait_ge(branch_out, 32)
                if b >= 2:
                    pe.wait_ge(pT_done, 2 * (b - 1))
                for h in range(GROUP):
                    tr(bank(6)[:, h * P:(h + 1) * P], qk[:, 2 * h:2 * h + 2, :], ident[:])
                tr(bank(7)[:, 0:P], qk[:, N_Q:N_Q + 2, :], ident[:]).then_inc(qkT_mm, 1)

            def scores(b, g):
                pe.wait_ge(qkT_done, 2 * (b + 1))
                if b >= 1:
                    pe.wait_ge(score_read, 2 * (b - 1) + g + 1)
                for h in range(GROUP):
                    last = mm(bank(2 + 2 * g, 2)[:, h * 2 * P:(h + 1) * 2 * P], qT[64 * g:64 * g + 64, h, :],
                              kT[64 * g:64 * g + 64, b * P:(b + 2) * P], start=True, stop=True)
                last.then_inc(score_mm, 1)

            def turn_prob(b, g):
                pe.wait_ge(prob_done, 2 * b + g + 1)
                if g == 0 and b + 1 < NT:
                    pe.wait_ge(qkT_done, 2 * (b + 2))
                if 2 * b + g >= 1:
                    pe.wait_ge(pT_done, 2 * b + g)
                for kb in range(2):
                    for h in range(GROUP):
                        last = tr(bank(6 + kb)[:, h * P:(h + 1) * P], prob[g][:, h, kb * P:(kb + 1) * P], ident[:])
                last.then_inc(pT_mm, 1)

            def values(b, g):
                pe.wait_ge(pT_done, 2 * b + g + 1)
                if b + 2 < NT:
                    pe.wait_ge(rope_done, b + 3)
                    pe.wait_ge(v_done, b + 3)
                if b >= 1:
                    pe.wait_ge(oT_done, 2 * (b - 1) + g + 1)
                for kb in range(2):
                    last = mm(bank(g)[64 * g:64 * g + 64, :], vrow[:, (b + kb) % 4, 64 * g:64 * g + 64],
                              pT[:, kb * HALF:(kb + 1) * HALF], start=(kb == 0), stop=(kb == 1))
                last.then_inc(pv_mm, 1)

            pe.wait_ge(wq_in, 16)
            pe.wait_ge(wkv_in, 16)
            for s in range(NT + 2):
                if 1 <= s <= NT:
                    turn_qk(s - 1)
                if s < NT:
                    project(s)
                if s >= 2:
                    turn_prob(s - 2, 0)
                if 1 <= s <= NT:
                    scores(s - 1, 0)
                if s >= 2:
                    values(s - 2, 0)
                    turn_prob(s - 2, 1)
                if 1 <= s <= NT:
                    scores(s - 1, 1)
                if s >= 2:
                    values(s - 2, 1)

            pe.wait_ge(wao_in, 32)
            pe.wait_ge(wlo_in, 16)
            pe.wait_ge(oT_done, 2 * NT)
            pe.wait_ge(lru_done, LM)
            for j in range(KD):
                if j >= 1:
                    pe.wait_ge(sgate_done, 4 * j)
                for k in range(KD):
                    n = j * KD + k
                    b, first, final = n % 2, k == 0, k == KD - 1
                    pe.wait_ge(gate_hi, n + 1)
                    for th in range(2):
                        for q in range(2):
                            mm(bank(2 * th + q), g_hi[b][:, q * P:(q + 1) * P], h_hi[b][:, th * HALF:(th + 1) * HALF],
                               start=first, stop=False)
                    pe.wait_ge(gate_lo, n + 1)
                    for th in range(2):
                        for q in range(2):
                            mm(bank(2 * th + q), g_lo[b][:, q * P:(q + 1) * P], h_hi[b][:, th * HALF:(th + 1) * HALF],
                               start=False, stop=False)
                            last = mm(bank(2 * th + q), g_hi[b][:, q * P:(q + 1) * P], h_lo[b][:, th * HALF:(th + 1) * HALF],
                                      start=False, stop=final)
                    last.then_inc(gate_mm, 1)
                if j == 0:
                    pe.wait_ge(pT_done, 2 * NT)
                else:
                    pe.wait_ge(merged_done, 2 * j)
                for th in range(2):
                    for q, (w, x_) in enumerate(((wao_sb, oT), (wlo_sb, lruT))):
                        for k in range(GROUP):
                            last = mm(bank(4 + 2 * th + q), w[:, k, j * P:(j + 1) * P], x_[:, k, th * HALF:(th + 1) * HALF],
                                      start=(k == 0), stop=(k == GROUP - 1))
                        last.then_inc(proj_mm, 1)

            pe.wait_ge(merged_done, 2 * KD)

            def router_T(t):
                pe.wait_ge(h2_done, t + 1)
                if t >= 1:
                    pe.wait_ge(h2T_done, t)
                for k in range(KD):
                    last = tr(bank(4, 2)[:, k * P:(k + 1) * P], h2[t % 2][:, k * P:(k + 1) * P], ident[:])
                last.then_inc(h2T_mm, 1)

            def router_mm(t):
                pe.wait_ge(h2T_done, t + 1)
                if t >= 2:
                    pe.wait_ge(logit_done, t - 1)
                for k in range(KD):
                    last = mm(bank(6 + t % 2)[:, 0:NE], h2T[:, k * P:(k + 1) * P], wrt[:, k, :],
                              start=(k == 0), stop=(k == KD - 1))
                last.then_inc(logit_mm, 1)

            for t in range(NT + 2):
                if t < NT:
                    if t >= 2:
                        pe.wait_ge(x2_done, t - 1)
                    pe.wait_ge(m_lo_done, t + 1)
                    for half in range(2):
                        for k in range(KD):
                            if t == 0 and k % 2 == 0:
                                pe.wait_ge(wo_lo_done, half * 4 + k // 2 + 1)
                            left = m_lo[:, k, t * P:(t + 1) * P]
                            right = slice(k * HALF, (k + 1) * HALF)
                            acc = bank(2 * (t % 2) + half)
                            mm(acc, m_hi[t % 2][:, k, :], wo_hi[half][:, right], start=(k == 0), stop=False)
                            mm(acc, left, wo_hi[half][:, right], start=False, stop=False)
                            last = mm(acc, m_hi[t % 2][:, k, :], wo_lo[half][:, right], start=False, stop=(k == KD - 1))
                    last.then_inc(wo_mm, 1)
                if t >= 2:
                    router_mm(t - 2)
                if 1 <= t <= NT:
                    router_T(t - 1)

            pe.wait_ge(mask_done, 1)
            for t in range(NT):
                for s in range(t + 1):
                    mm(bank(0)[:, t * NE:(t + 1) * NE], (tri_b if s == t else ones_b)[:], mask_b[:, s, :],
                       start=(s == 0), stop=(s == t))
            for s in range(NT):
                last = mm(bank(1)[:, 0:NE], ones_b[:], mask_b[:, s, :], start=(s == 0), stop=(s == NT - 1))
            last.then_inc(rank_mm, 1)
            pe.wait_ge(columns_done, 1)
            for q in range(3):
                last = tr(bank(1)[0:1, q * P:(q + 1) * P], tab_c[:, q:q + 1], ident[:])
            last.then_inc(columns_mm, 1)

            pe.wait_ge(table_done, 1)

            def chunk_meta(e):
                for t in range(NT):
                    last = mm(bank(7)[:, 0:NMETA], onehot[:, t, :], meta[:, ds(e * (NT * NMETA) + t * NMETA, NMETA)],
                              start=(t == 0), stop=(t == NT - 1))
                last.then_inc(meta_mm, 1)

            def chunk_rowsT(u):
                for k in range(KD):
                    last = tr(bank(6, 2)[:, k * P:(k + 1) * P], rows_g[u][:, k * P:(k + 1) * P], ident[:])
                last.then_inc(rowsT_mm, 1)

            total = pe.value_load(ends[0:1, NE - 1:NE], min_val=1, max_val=MAXC)
            first_e, second_e = load_slots(pe, 0)[0], load_slots(pe, 1)[0]
            pe.sem_inc(sub_mm, NBUF)
            pe.wait_ge(onehot_done, 1)
            chunk_meta(first_e)
            pe.wait_ge(onehot_done, 2)
            pe.wait_ge(idx_done, 1)
            chunk_meta(second_e)
            pe.wait_ge(rows_in[0], 16)
            pe.wait_ge(idx_done, 2)
            chunk_rowsT(0)
            pe.wait_ge(bias_done, 1)
            pe.wait_ge(sel_done, 4)
            with pe.Fori(0, MAXC // 2) as pair:
                for u in range(2):
                    j = pair * 2 + u
                    with pe.If(j < total):
                        e, tail, f, _, _, _ = load_step(pe, j)
                        e_ahead, _, _ = load_slots(pe, j + 2)
                        BIAS_COL = (0, D, HALF, D + HALF, 2 * D, 2 * D + HALF)

                        def piece(n):
                            i, k0 = sub_unit(n)
                            hi, lo = (rows_hi, rows_lo) if i < 4 else (act_hi, act_lo)
                            pe.wait_ge(hi_done, f * SUBS + n + 1)
                            for q in range(2):
                                ks = slice((k0 + q) * P, (k0 + q + 1) * P)
                                wh = w_hi[:, n % NBUF, q * HALF:(q + 1) * HALF]
                                mm(bank(i), hi[:, ks], wh, start=(k0 + q == 0), stop=False)
                                mm(bank(i), lo[:, ks], wh, start=False, stop=False)
                            if n in ON_POOL:
                                pe.wait_ge(lo_pool, f * len(ON_POOL) + ON_POOL.index(n) + 1)
                            else:
                                pe.wait_ge(lo_dve, f * (SUBS - len(ON_POOL)) + n - sum(x < n for x in ON_POOL) + 1)
                            for q in range(2):
                                last = mm(bank(i), hi[:, (k0 + q) * P:(k0 + q + 1) * P], w_lo[:, n % NBUF, q * HALF:(q + 1) * HALF],
                                          start=False, stop=False)
                            last.then_inc(sub_mm, 1)
                            if k0 + 2 == KD:
                                if i == 0:
                                    pe.wait_ge(sel_ready, j + 1)
                                mm(bank(i), sel_cur[0:96, u, :], bias3[0:96, BIAS_COL[i]:BIAS_COL[i] + HALF],
                                   start=False, stop=True).then_inc(unit_mm[i], 1)

                        def tail_product(b_, units, stat_of, ks):
                            for k in ks:
                                for q in range(QUART):
                                    i, c = units[q // 2], QC * (q % 2)
                                    dst = bank(b_)[TAIL * q:TAIL * (q + 1), 0:QC]
                                    if k == 0 and q % 2 == 0:
                                        pe.wait_ge(w_arrived[i], e * 16 + 16)
                                    mm(dst, stat_of(k, q), wu[i][:, k, c:c + QC], start=(k == 0), stop=False)
                            if ks[-1] == KD - 1:
                                pe.wait_ge(sel_ready, j + 1)
                                for q in range(QUART):
                                    i, c = units[q // 2], QC * (q % 2)
                                    last = mm(bank(b_)[TAIL * q:TAIL * (q + 1), 0:QC], sel_cur[0:96, u, 0:TAIL],
                                              bias3[0:96, BIAS_COL[i] + c:BIAS_COL[i] + c + QC], start=False, stop=True)
                                    if q % 2 == 1:
                                        last.then_inc(unit_mm[i], 1)

                        def next_meta():
                            pe.wait_ge(onehot_done, j + 3)
                            chunk_meta(e_ahead)

                        def next_rows():
                            pe.wait_ge(rows_in[1 - u], (pair + 1 + u) * 16)
                            pe.wait_ge(idx_done, j + 3)
                            chunk_rowsT(1 - u)

                        pe.wait_ge(rowsT_done, j + 1)
                        with pe.If(tail < 1):
                            pe.wait_ge(rows_lo_done, f + 1)
                            for n in range(SUBS):
                                if n == 8:
                                    next_meta()
                                if n in ACT_T:
                                    half = ACT_T.index(n)
                                    pe.wait_ge(act_done, j * 2 + half + 2)
                                    for k in range(4):
                                        last = tr(bank(2 * half)[:, k * P:(k + 1) * P], uclip[:, half, k * P:(k + 1) * P], ident[:])
                                    last.then_inc(actT_mm, 1)
                                if n == 20:
                                    next_rows()
                                if n == 16:
                                    pe.wait_ge(y_done, j * 2 + 1)
                                if n in (16, 20):
                                    pe.wait_ge(act_lo_done, f * 2 + (n - 16) // 4 + 1)
                                piece(n)
                        with pe.If(tail > 0):
                            tail_product(0, (0, 2), lambda k, q: rowsT_tail[:, k * TAIL:(k + 1) * TAIL], range(KD))
                            next_meta()
                            tail_product(1, (1, 3), lambda k, q: rowsT_tail[:, k * TAIL:(k + 1) * TAIL], range(KD))
                            next_rows()
                            for half in range(2):
                                pe.wait_ge(act_done, j * 2 + half + 2)
                                tr(bank(2 * half)[:, 0:P], uclip[:, 0, half * P:(half + 1) * P], ident[:]).then_inc(actT_mm, 1)
                                pe.wait_ge(actT_done, j * 2 + half + 1)
                                if half == 0:
                                    pe.wait_ge(y_done, j * 2 + 1)
                                tail_product(4, (4, 5), lambda k, q: actT_tail[:, half * P + TAIL * (k // 2):half * P + TAIL * (k // 2 + 1)],
                                             range(half, KD, 2))

        @block.scalar
        def _(act):
            loads = [
                (pos_i[:], positions[0].rearrange("(t p) -> p t", p=P)),
                (freq[:], inv_freq[None, :].to_broadcast([P, HD // 2])),
                (convb[:], conv_b[0].rearrange("(m p) -> p m", p=P)),
                (brg[:], b_rg[0].rearrange("(m p) -> p m", p=P)),
                (big[:], b_ig[0].rearrange("(m p) -> p m", p=P)),
                (lam[:], lru_lambda[0].rearrange("(m p) -> p m", p=P)),
                (sink[:], attn_sinks[0][None, :].to_broadcast([P, N_Q])),
                (wrt[:], w_router[0].rearrange("(k p) e -> p k e", p=P)),
                (brt[:], b_router[0][None, :].to_broadcast([P, NE])),
            ] + [(convw[:, c, :], conv_w[0, c].rearrange("(m p) -> p m", p=P)) for c in range(CONV)]
            assert len(loads) == N_CONST
            with nc.allow_non_contiguous_dma("small vectors, one element per partition"):
                act.dma_start(gmix[:], norm_mix_g[0].rearrange("(k p) -> p k", p=P)).then_inc(gmix_in, 16)
            act.wait_ge(eps_built, 1)
            for t in range(NT):
                act.wait_ge(x_in[t], 16)
                act.activation(region_a[:, 0:D], xin[:, t, :], ACT.Square, accum_out=ssq[:, 0, t:t + 1]).then_inc(ssq_done, 1)
                act.wait_ge(ssq_done, t + 1)
                act.activation(rms[:, 0, t:t + 1], ssq[:, 0, t:t + 1], ACT.Sqrt, bias=eps[:], scale=1.0 / D).then_inc(rms_done, 1)
            with nc.allow_non_contiguous_dma("small vectors, one element per partition"):
                for dst, src in loads:
                    act.dma_start(dst, src).then_inc(consts_in, 16)
            act.wait_ge(sin_in, 1)
            act.activation(sin, sin, ACT.Sin).then_inc(sin_done, 1)
            act.activation(cos, cos, ACT.Sin).then_inc(sin_done, 1)
            act.wait_ge(clam_exp, 1)
            act.activation(clam[:, 1, :], clam[:, 0, :], ACT.Exp, scale=-1.0).then_inc(clam_exp, 1)
            for n in range(16):
                m, th = (n // 2) % LM, n % 2
                act.wait_ge(branch_mm, n + 1)
                if n < 8:
                    act.activation(xr[:, m, 3 + th * HALF:3 + (th + 1) * HALF], bank(4 + n % 4), ACT.Copy).then_inc(branch_out, 1)
                else:
                    act.activation(lruT[:, m, th * HALF:(th + 1) * HALF], bank(4 + n % 4), ACT.Gelu_apprx_tanh).then_inc(branch_out, 1)
            for n in range(16, 32):
                m, g, th = (n - 16) // 4, (n // 2) % 2, n % 2
                act.wait_ge(branch_mm, n + 1)
                dst = xr[:, m, 3 + th * HALF:3 + (th + 1) * HALF] if g == 0 else igate[:, m, th * HALF:(th + 1) * HALF]
                act.activation(dst, bank(4 + n % 4), ACT.Sigmoid, bias=(brg, big)[g][:, m:m + 1]).then_inc(branch_out, 1)
            act.wait_ge(branch_out, 32)
            for m in range(LM):
                act.wait_ge(ix_done, m + 1)
                act.activation(xc[:, m, :], xr[:, m, 3:3 + SEQ], ACT.Exp, scale=clam[:, 5, m:m + 1]).then_inc(expa_done, 1)
                act.wait_ge(expa_done, 2 * m + 1)
                act.activation(xr[:, m, 3:3 + SEQ], xr[:, m, 3:3 + SEQ], ACT.Tanh, scale=clam[:, 5, m:m + 1]).then_inc(expa_done, 1)
            for m in range(LM):
                act.wait_ge(om_done, m + 1)
                act.activation(xr[:, m, 3:3 + SEQ], xr[:, m, 3:3 + SEQ], ACT.Sqrt, scale=-1.0).then_inc(sqrt_done, 1)
            for s in range(NT + 2):
                if 1 <= s <= NT:
                    b = s - 1
                    act.wait_ge(qkT_mm, b + 1)
                    if b >= 1:
                        act.wait_ge(score_mm, 2 * b)
                    act.activation(qT, bank(6), ACT.Copy).then_inc(qkT_done, 1)
                    act.activation(kT[:, (b + 1) * P:(b + 2) * P], bank(7)[:, 0:P], ACT.Copy).then_inc(qkT_done, 1)
                if s >= 2:
                    b = s - 2
                    for g in range(N_KV):
                        act.wait_ge(pT_mm, 2 * b + g + 1)
                        if 2 * b + g >= 1:
                            act.wait_ge(pv_mm, 2 * b + g)
                        act.activation(pT, bank(6, 2), ACT.Copy).then_inc(pT_done, 1)
                        act.wait_ge(pv_mm, 2 * b + g + 1)
                        act.activation(oT[64 * g:64 * g + 64, :, b * P:(b + 1) * P],
                                       bank(g)[64 * g:64 * g + 64, :].rearrange("p (h q) -> p h q", h=GROUP),
                                       ACT.Copy).then_inc(oT_done, 1)
                if 1 <= s <= NT:
                    b = s - 1
                    for g in range(N_KV):
                        act.wait_ge(negm_done, 2 * b + g + 1)
                        for h in range(GROUP):
                            gh = GROUP * g + h
                            act.activation(prob[g][:, h, :], prob[g][:, h, :], ACT.Exp, bias=negm[:, gh:gh + 1],
                                           accum_out=sume[:, gh:gh + 1])
                        act.activation(esink[:, GROUP * g:GROUP * (g + 1)], esink[:, GROUP * g:GROUP * (g + 1)],
                                       ACT.Exp).then_inc(exp_done, 1)
            act.wait_ge(lru_done, LM)
            act.wait_ge(pT_mm, 2 * NT)
            act.wait_ge(pv_mm, 2 * NT)

            def gate_high(n):
                j, k, b = n // KD, n % KD, n % 2
                if n % (2 * KD) == 0:
                    act.wait_ge(ga_in[j // 2], 16)
                    act.wait_ge(gl_in[j // 2], 16)
                if n >= 2:
                    act.wait_ge(gate_mm, n - 1)
                act.activation(h_hi[b][:], hT[:, k, :], ACT.Copy)
                c = (j % 2) * P
                act.activation(g_hi[b][:, 0:P], ga_sb[j // 2][:, k, c:c + P], ACT.Copy)
                act.activation(g_hi[b][:, P:2 * P], gl_sb[j // 2][:, k, c:c + P], ACT.Copy).then_inc(gate_hi, 1)

            for n in range(KD * KD):
                gate_high(n)
                if n % KD == KD - 1:
                    j = n // KD
                    act.wait_ge(gate_mm, n + 1)
                    if j >= 1:
                        act.wait_ge(merged_done, 2 * j)
                    for th in range(2):
                        for q in range(2):
                            act.activation(sgate[th][q], bank(2 * th + q), ACT.Sigmoid).then_inc(sgate_done, 1)
            def h2T_out(t):
                act.wait_ge(h2T_mm, t + 1)
                if t >= 1:
                    act.wait_ge(logit_mm, t)
                act.activation(h2T, bank(4, 2), ACT.Copy).then_inc(h2T_done, 1)

            def wo_high(q):
                half = q // 4
                if q == 0:
                    act.wait_ge(wo_in[0], 16)
                    act.wait_ge(gate_mm, KD * KD)
                if q == 4:
                    act.wait_ge(wo_in[1], 16)
                    act.wait_ge(proj_mm, 4 * KD)
                cols = slice((q % 4) * D, (q % 4 + 1) * D)
                act.activation(wo_hi[half][:, cols], wo_sb[half].rearrange("p k n -> p (k n)")[:, cols],
                               ACT.Copy).then_inc(wo_hi_done, 1)

            def merged_high(t):
                if t == 0:
                    act.wait_ge(merged_done, 2 * KD)
                if t >= 2:
                    act.wait_ge(wo_mm, t - 1)
                act.activation(m_hi[t % 2][:], merged[:, :, t * P:(t + 1) * P], ACT.Copy).then_inc(m_hi_done, 1)

            for q in range(4):
                wo_high(q)
            merged_high(0)
            for q in range(4, 8):
                wo_high(q)
            merged_high(1)
            for t in range(NT):
                act.wait_ge(x2_done, t + 1)
                if t >= 2:
                    act.wait_ge(h2T_mm, t - 1)
                    act.wait_ge(h2_out[t % 2], 16 * (t // 2))
                act.activation(h2[t % 2], xb[t % 2], ACT.Square, accum_out=ssq[:, 1, t:t + 1]).then_inc(ssq_done, 1)
                act.wait_ge(ssq_done, NT + t + 1)
                act.activation(rms[:, 1, t:t + 1], ssq[:, 1, t:t + 1], ACT.Sqrt, bias=eps[:], scale=1.0 / D).then_inc(rms_done, 1)
                if t + 2 < NT:
                    merged_high(t + 2)
                if t >= 1:
                    h2T_out(t - 1)
            h2T_out(NT - 1)
            act.wait_ge(gexp_in, 1)
            act.activation(gate4, gate4, ACT.Exp).then_inc(gexp_done, 1)

            act.wait_ge(table_done, 1)
            total = act.value_load(ends[0:1, NE - 1:NE], min_val=1, max_val=MAXC)

            def rowsT_full():
                act.activation(rows_hi[:], bank(6, 2), ACT.Copy).then_inc(rowsT_done, 1)

            def high(n, f, e):
                i, k0 = sub_unit(n)
                if k0 == 0:
                    wait_reg(act, w_arrived[i], e * 16 + 16)
                act.wait_ge(sub_mm, f * SUBS + n + 1)
                act.activation(w_hi[:, n % NBUF, :], place[i][:, k0 * HALF:(k0 + 2) * HALF], ACT.Copy).then_inc(hi_done, 1)

            act.sem_inc(y_done)
            act.wait_ge(rowsT_mm, 1)
            rowsT_full()
            for n in range(NBUF):
                high(n, 0, 0)
            with act.Fori(0, MAXC // 2) as pair:
                for u in range(2):
                    j = pair * 2 + u
                    with act.If(j < total):
                        e, tail, f, e_next, t_next, f_next = load_step(act, j)

                        def sigmoid(dst, src, half):
                            act.wait_ge(gclip_done, j * 2 + half + 1)
                            act.activation(dst, src, ACT.Sigmoid, scale=ALPHA).then_inc(gsig_done, 1)

                        def next_rowsT():
                            wait_reg(act, rowsT_mm, j + 2)
                            with act.If(t_next < 1):
                                rowsT_full()
                            with act.If(t_next > 0):
                                act.activation(rowsT_tail.rearrange("p (k s) -> p k s", k=KD),
                                               bank(6, 2).rearrange("p (k s) -> p k s", k=KD)[:, :, 0:TAIL],
                                               ACT.Copy).then_inc(rowsT_done, 1)

                        def actT_out(dst, src, half):
                            act.wait_ge(actT_mm, j * 2 + half + 1)
                            act.activation(dst, src, ACT.Copy).then_inc(actT_done, 1)

                        def outputs(width, banks, last_unit):
                            for half in range(2):
                                with act.If(t_next < 1):
                                    for n in (2 * half, 2 * half + 1):
                                        high(n, f_next, e_next)
                                if half == 0:
                                    wait_reg(act, cur_done, j + 1)
                                    wait_reg(act, added, j * 16 + 16)
                                act.wait_ge(unit_mm[last_unit[half]], j + 1)
                                act.activation(yrow[u][:, half * width:(half + 1) * width], banks[half], ACT.Copy,
                                               scale=w_cur[:, u:u + 1]).then_inc(y_done, 1)

                        with act.If(tail < 1):
                            for n in range(NBUF, SUBS):
                                high(n, f, e)
                                if n == 8:
                                    sigmoid(gsig, gclip, 0)
                                if n == 15:
                                    actT_out(act_hi[:, 0:HALF], bank(0), 0)
                                if n == 17:
                                    sigmoid(gsig, gclip, 1)
                                if n == 21:
                                    actT_out(act_hi[:, HALF:D], bank(2), 1)
                            next_rowsT()
                            outputs(HALF, (bank(4), bank(5)), (4, 5))
                        with act.If(tail > 0):
                            for half in range(2):
                                sigmoid(gsig[:, half * P:(half + 1) * P], gclip[:, half * P:(half + 1) * P], half)
                            next_rowsT()
                            for half in range(2):
                                actT_out(actT_tail[:, half * P:(half + 1) * P], bank(2 * half)[:, 0:P], half)
                            outputs(P, (bank(4)[:, 0:P], bank(4)[:, P:2 * P]), (5, 5))
            for t in range(NT):
                act.wait_ge(acc_in[t], 16)
                act.activation(fjunk, fin[t], ACT.Square, accum_out=ssq[:, 2, t:t + 1]).then_inc(fssq, 1)
                act.wait_ge(fssq, t + 1)
                act.activation(rms[:, 2, t:t + 1], ssq[:, 2, t:t + 1], ACT.Sqrt, bias=eps[:], scale=1.0 / D).then_inc(frms, 1)

        @block.gpsimd
        def _(pool):
            g = nc.gpsimd
            steps = [0]

            def then(ins):
                steps[0] += 1
                ins.then_inc(pool_step, 1)
                pool.wait_ge(pool_step, steps[0])

            then(g.memset(ident[:], 0.0))
            g.affine_select(out=ident[:], in_=ident[:], compare_op=ALU.not_equal, fill=1.0, base=0,
                            pattern=[[-1, P]], channel_multiplier=1).then_inc(ident_built, 1)
            g.memset(eps[:], EPS).then_inc(eps_built, 1)
            then(g.memset(bd, 0.0))
            with nc.allow_non_contiguous_dma("64-wide diagonal blocks"):
                for q, w in enumerate((w_rg, w_ig)):
                    wv = w[0].rearrange("(m h) i j -> h i m j", h=2)
                    for h in range(2):
                        g.dma_start(bd[64 * h:64 * h + 64, q, :, 64 * h:64 * h + 64], wv[h]).then_inc(bd_in, 16)
            for m_ in (mask[:], mask_first):
                then(g.memset(m_, 0.0))
                then(g.affine_select(out=m_, in_=m_, compare_op=ALU.is_ge, fill=NEG_INF, base=P,
                                     pattern=[[-1, 2 * P]], channel_multiplier=1))
                ins = g.affine_select(out=m_, in_=m_, compare_op=ALU.is_ge, fill=NEG_INF, base=-1,
                                      pattern=[[1, 2 * P]], channel_multiplier=-1)
                if m_ is mask_first:
                    then(ins)
                else:
                    ins.then_inc(small_built, 1)
            g.affine_select(out=mask_first, in_=mask_first, compare_op=ALU.is_ge, fill=NEG_INF, base=-P,
                            pattern=[[1, 2 * P]], channel_multiplier=0).then_inc(small_built, 1)
            g.memset(ones_b[:], 1.0).then_inc(small_built, 1)
            then(g.memset(tri_b[:], 1.0))
            g.affine_select(out=tri_b[:], in_=tri_b[:], compare_op=ALU.is_ge, fill=0.0, base=-1,
                            pattern=[[1, P]], channel_multiplier=-1).then_inc(small_built, 1)
            for dst, pattern, mult in ((iota_e, [[1, NE]], 0), (iota_p, [[0, 1]], 1),
                                       (iota_t, [[P, NT]], 0)):
                g.iota(dst[:], pattern=pattern, base=0, channel_multiplier=mult,
                       allow_small_or_imprecise_dtypes=True).then_inc(small_built, 1)
            g.memset(row_next[:], 0).then_inc(small_built, 1)
            for q in range(QUART):
                then(g.memset(quart[TAIL * q:TAIL * (q + 1), :], float(q)))
            for m in range(LM):
                pool.wait_ge(branch_out, 16 + 4 * (m + 1))
                g.tensor_tensor(out=igate[:, m, :], in0=igate[:, m, :], in1=xc[:, m, :], op=ALU.mult).then_inc(ix_done, 1)
            pool.wait_ge(lru_done, LM)
            for q in range(3):
                g.dma_start(bstage[32 * q:32 * q + 32, 0:2 * D], b_gate_up[0]).then_inc(bias_in, 16)
                g.dma_start(bstage[32 * q:32 * q + 32, 2 * D:3 * D], b_down[0]).then_inc(bias_in, 16)
            pool.wait_ge(merged_done, 2 * KD)
            pool.wait_ge(bias_done, 1)
            g.dma_start(gffn, norm_ffn_g[0][None, :].to_broadcast([P, D])).then_inc(gffn_in, 16)
            for t in range(2):
                g.dma_start(xb[t], x_t[t]).then_inc(xb_in[t], 16)
            for t in range(NT):
                pool.wait_ge(x2_done, t + 1)
                g.dma_start(acc_t[t], xb[t % 2]).then_inc(acc_out[t % 2], 16)
                pool.wait_ge(h2_done, t + 1)
                g.dma_start(h2_t[t], h2[t % 2]).then_inc(h2_out[t % 2], 16)
                if t + 2 < NT:
                    pool.wait_ge(acc_out[t % 2], 16 * (t // 2 + 1))
                    g.dma_start(xb[t % 2], x_t[t + 2]).then_inc(xb_in[t % 2], 16)
            for q in range(2):
                pool.wait_ge(acc_out[q], 16 * (NT // 2))
                pool.wait_ge(h2_out[q], 16 * (NT // 2))
            pool.wait_ge(logit_mm, NT)
            g.iota(iota_s, pattern=[[1, SEQ]], base=0, channel_multiplier=0,
                   allow_small_or_imprecise_dtypes=True).then_inc(iota_built, 1)
            g.memset(sel[0:96, :], 0.0).then_inc(sel_done, 1)
            pool.wait_ge(sel_done, 1)
            for q in range(3):
                v = sel[32 * q:32 * q + 32, :].rearrange("p (e m) -> p e m", e=NE)
                g.affine_select(out=v, in_=v, compare_op=ALU.not_equal, fill=1.0, base=0,
                                pattern=[[-1, NE], [0, P]], channel_multiplier=1).then_inc(sel_done, 1)
                pool.wait_ge(sel_done, q + 2)
            for half in (slice(0, HALF), slice(HALF, D)):
                g.dma_start(gfin[:, half], norm_final_g[None, half].to_broadcast([P, HALF])).then_inc(added, 16)

            def gather(u):
                g.indirect_dma_start(out=rows_g[u], out_offset=None, in_=h2_rows,
                                     in_offset=bass.IndirectOffsetOnAxis(ap=row_next[:, u, 0:1], axis=0),
                                     bounds_check=SEQ - 1, oob_is_err=False).then_inc(rows_in[u], 16)

            def add(u, dst, col, width, rows):
                g.indirect_dma_start(out=dst, out_offset=bass.IndirectOffsetOnAxis(ap=row_cur[:, u, col:col + 1], axis=0),
                                     in_=yrow[u][:, 0:width], in_offset=None, bounds_check=rows - 1, oob_is_err=False,
                                     compute_op=ALU.add).then_inc(added, 16)

            pool.wait_ge(table_done, 1)
            total = pool.value_load(ends[0:1, NE - 1:NE], min_val=1, max_val=MAXC)
            for u in range(2):
                pool.wait_ge(idx_done, u + 1)
                gather(u)
            with pool.Fori(0, MAXC // 2) as pair:
                for u in range(2):
                    j = pair * 2 + u
                    with pool.If(j < total):
                        _, tail, f, _, _, _ = load_step(pool, j)

                        def next_gather():
                            wait_reg(pool, idx_done, j + 3)
                            wait_reg(pool, rowsT_mm, j + 1)
                            gather(u)

                        def outputs_are_there():
                            wait_reg(pool, y_done, j * 2 + 3)
                            wait_reg(pool, cur_done, j + 1)
                            wait_reg(pool, added, j * 16 + 32)

                        with pool.If(tail < 1):
                            for n in ON_POOL:
                                i, k0 = sub_unit(n)
                                wait_reg(pool, hi_done, f * SUBS + n + 1)
                                g.tensor_tensor(out=w_lo[:, n % NBUF, :], in0=place[i][:, k0 * HALF:(k0 + 2) * HALF],
                                                in1=w_hi[:, n % NBUF, :].bitcast(f32), op=ALU.subtract).then_inc(lo_pool, 1)
                                if n == ON_POOL[2]:
                                    next_gather()
                            outputs_are_there()
                            add(u, acc_rows, 0, D, SEQ)
                        with pool.If(tail > 0):
                            next_gather()
                            outputs_are_there()
                            add(u, acc_rows.rearrange("t (q c) -> (t q) c", q=QUART), 1, QC, SEQ * QUART)

        @block.vector
        def _(dve):
            v = nc.vector
            steps = [0]

            def then(ins):
                steps[0] += 1
                ins.then_inc(dve_step, 1)
                dve.wait_ge(dve_step, steps[0])

            def bc(ap, shape):
                return ap.to_broadcast(shape)

            def xnorm(t):
                dve.wait_ge(rms_done, t + 1)
                v.reciprocal(rinv[:, 0, t:t + 1], rms[:, 0, t:t + 1]).then_inc(rinv_done, 1)
                dve.wait_ge(rinv_done, t + 1)
                v.tensor_scalar(xin[:, t, :], xin[:, t, :], rinv[:, 0, t:t + 1], None, ALU.mult).then_inc(xn_done, 1)

            def hT_out(t):
                for q in range(2):
                    dve.wait_ge(xT_done, 2 * t + q + 1)
                    v.tensor_tensor(out=hT[:, 4 * q:4 * q + 4, t * P:(t + 1) * P],
                                    in0=bank(2 * (t % 2) + q).rearrange("p (k n) -> p k n", k=4),
                                    in1=bc(gmix[:, 4 * q:4 * q + 4, None], [P, 4, P]), op=ALU.mult).then_inc(hT_done, 1)

            for t in range(NT + 1):
                if t < NT:
                    xnorm(t)
                if t == 1:
                    dve.wait_ge(gmix_in, 16)
                if t >= 1:
                    hT_out(t - 1)
            dve.wait_ge(consts_in, 16 * N_CONST)
            dve.wait_ge(small_built, N_BUILT)
            then(v.tensor_copy(pos_f[:], pos_i[:]))
            ang, turn = unit_view(region_a[:, 0:NT * 32], NT), unit_view(region_a[:, NT * 32:2 * NT * 32], NT)
            dve.wait_ge(ssq_done, NT)
            then(v.tensor_tensor(out=ang, in0=bc(pos_f[:, :, None], [P, NT, 32]), in1=bc(freq[:, None, :], [P, NT, 32]), op=ALU.mult))
            for dst, quarter in ((sin, 0.0), (cos, 0.25)):
                then(v.tensor_scalar(turn, ang, 1.0 / (2 * 3.141592653589793), quarter, ALU.mult, ALU.add))
                then(v.tensor_scalar(turn, turn, MAGIC, None, ALU.add))
                then(v.tensor_scalar(turn, turn, MAGIC, None, ALU.subtract))
                src = ang
                for c in TWO_PI_PARTS:
                    then(v.scalar_tensor_tensor(out=dst, in0=turn, scalar=-c, in1=src, op0=ALU.mult, op1=ALU.add))
                    src = dst
                pi = 3.1415925
                then(v.tensor_scalar(dst, dst, quarter * 2 * 3.141592653589793, pi, ALU.add, ALU.min))
                ins = v.tensor_scalar(dst, dst, -pi, None, ALU.max)
                if quarter:
                    ins.then_inc(sin_in, 1)
                else:
                    then(ins)
            then(v.tensor_scalar(clam[:, 2, :], lam[:], -1.0, None, ALU.mult))
            v.tensor_tensor(out=clam[:, 0, :], in0=lam[:], in1=clam[:, 2, :], op=ALU.max).then_inc(clam_exp, 1)
            dve.wait_ge(clam_exp, 2)
            then(v.tensor_scalar(clam[:, 3, :], clam[:, 1, :], 2.0, None, ALU.add))
            then(v.reciprocal(clam[:, 4, :], clam[:, 3, :]))
            then(v.tensor_tensor(out=clam[:, 1, :], in0=clam[:, 1, :], in1=clam[:, 4, :], op=ALU.mult))
            then(v.tensor_tensor(out=clam[:, 3, :], in0=clam[:, 1, :], in1=clam[:, 1, :], op=ALU.mult))
            then(v.memset(clam[:, 4, :], 0.0))
            for q in range(9, 0, -1):
                then(v.scalar_tensor_tensor(out=clam[:, 4, :], in0=clam[:, 4, :], scalar=1.0 / (2 * q + 1), in1=clam[:, 3, :],
                                            op0=ALU.add, op1=ALU.mult))
            then(v.scalar_tensor_tensor(out=clam[:, 4, :], in0=clam[:, 4, :], scalar=1.0, in1=clam[:, 1, :], op0=ALU.add, op1=ALU.mult))
            then(v.tensor_scalar(clam[:, 2, :], clam[:, 2, :], 0.0, -LRU_C, ALU.max, ALU.mult))
            then(v.scalar_tensor_tensor(out=clam[:, 5, :], in0=clam[:, 4, :], scalar=-2.0 * LRU_C, in1=clam[:, 2, :],
                                        op0=ALU.mult, op1=ALU.add))
            v.memset(kT[:, 0:P], 0.0)
            v.memset(vrow[:, 0, :], 0.0)
            dve.wait_ge(xT_done, 2 * NT)
            then(v.memset(xr[:, :, 0:3], 0.0))
            for m in range(LM):
                dve.wait_ge(branch_out, 2 * (m + 1))
                then(v.tensor_scalar(xc[:, m, :], xr[:, m, 3:3 + SEQ], convw[:, 3, m:m + 1], convb[:, m:m + 1], ALU.mult, ALU.add))
                for c in (2, 1, 0):
                    ins = v.scalar_tensor_tensor(out=xc[:, m, :], in0=xr[:, m, c:c + SEQ], scalar=convw[:, c, m:m + 1],
                                                 in1=xc[:, m, :], op0=ALU.mult, op1=ALU.add)
                    if c:
                        then(ins)
                    else:
                        ins.then_inc(conv_done, 1)
            a2 = region_a[:, A_COLS - SEQ:A_COLS]
            for m in range(LM):
                dve.wait_ge(expa_done, 2 * (m + 1))
                if m >= 1:
                    dve.wait_ge(om_done, m)
                then(v.tensor_tensor(out=a2, in0=xc[:, m, :], in1=xc[:, m, :], op=ALU.mult))
                v.scalar_tensor_tensor(out=xr[:, m, 3:3 + SEQ], in0=a2, scalar=1.0, in1=xr[:, m, 3:3 + SEQ],
                                       op0=ALU.add, op1=ALU.mult).then_inc(om_done, 1)

            def recur(m):
                dve.wait_ge(sqrt_done, m + 1)
                then(v.tensor_tensor(out=xr[:, m, 3:3 + SEQ], in0=xr[:, m, 3:3 + SEQ], in1=igate[:, m, :], op=ALU.mult))
                then(v.tensor_tensor_scan(igate[:, m, :], xc[:, m, :], xr[:, m, 3:3 + SEQ], 0.0, ALU.mult, ALU.add))
                v.tensor_tensor(out=lruT[:, m, :], in0=lruT[:, m, :], in1=igate[:, m, :], op=ALU.mult).then_inc(lru_done, 1)

            dve.wait_ge(sin_done, 2)
            for s in range(NT + 1):
                if s < NT:
                    dve.wait_ge(qkv_mm, s + 1)
                    if s >= 1:
                        dve.wait_ge(qkT_mm, s)
                        dve.wait_ge(rope_done, s)
                    nh = N_Q + N_KV
                    src = psum[:, 0:nh * HD].rearrange("p (h d) -> p h d", d=HD)
                    t1, t2 = src[:, :, 0:32], src[:, :, 32:64]
                    c_, s_ = bc(cos[:, s:s + 1, :], [P, nh, 32]), bc(sin[:, s:s + 1, :], [P, nh, 32])
                    v.tensor_tensor(out=ropa, in0=t1, in1=c_, op=ALU.mult)
                    then(v.tensor_tensor(out=ropb, in0=t2, in1=s_, op=ALU.mult))
                    then(v.tensor_tensor(out=qk[:, :, 0:32], in0=ropa, in1=ropb, op=ALU.subtract))
                    v.tensor_tensor(out=ropa, in0=t2, in1=c_, op=ALU.mult)
                    then(v.tensor_tensor(out=ropb, in0=t1, in1=s_, op=ALU.mult))
                    v.tensor_tensor(out=qk[:, :, 32:64], in0=ropa, in1=ropb, op=ALU.add).then_inc(rope_done, 1)
                    v.tensor_copy(vrow[:, (s + 1) % 4, :], bank(1)[:, KVW:2 * KVW]).then_inc(v_done, 1)
                if s < LM:
                    recur(s)
                if s >= 1:
                    b = s - 1
                    for g in range(N_KV):
                        hs = slice(GROUP * g, GROUP * (g + 1))
                        dve.wait_ge(score_mm, 2 * b + g + 1)
                        if b >= 1:
                            dve.wait_ge(pT_mm, 2 * (b - 1) + g + 1)
                        v.scalar_tensor_tensor(out=prob[g], in0=bank(2 + 2 * g, 2).rearrange("p (h k) -> p h k", h=GROUP),
                                               scalar=HD ** -0.5, in1=bc((mask[:] if b else mask_first)[:, None, :], [P, GROUP, 2 * P]),
                                               op0=ALU.mult, op1=ALU.add).then_inc(score_read, 1)
                        dve.wait_ge(score_read, 2 * b + g + 1)
                        then(v.tensor_reduce(out=mx[:, hs], in_=prob[g], axis=AX, op=ALU.max))
                        then(v.tensor_tensor(out=mx[:, hs], in0=mx[:, hs], in1=sink[:, hs], op=ALU.max))
                        then(v.tensor_scalar(negm[:, hs], mx[:, hs], -1.0, None, ALU.mult))
                        v.tensor_tensor(out=esink[:, hs], in0=sink[:, hs], in1=negm[:, hs], op=ALU.add).then_inc(negm_done, 1)
                    for g in range(N_KV):
                        hs = slice(GROUP * g, GROUP * (g + 1))
                        dve.wait_ge(exp_done, 2 * b + g + 1)
                        then(v.tensor_tensor(out=rden[:, hs], in0=sume[:, hs], in1=esink[:, hs], op=ALU.add))
                        then(v.reciprocal(rden[:, hs], rden[:, hs]))
                        v.tensor_tensor(out=prob[g], in0=prob[g], in1=bc(rden[:, hs, None], [P, GROUP, 2 * P]),
                                        op=ALU.mult).then_inc(prob_done, 1)
            def gate_low(n):
                j, k, b = n // KD, n % KD, n % 2
                dve.wait_ge(gate_hi, n + 1)
                v.tensor_tensor(out=h_lo[b][:], in0=hT[:, k, :], in1=h_hi[b][:].bitcast(f32), op=ALU.subtract)
                c = (j % 2) * P
                for q, w in enumerate((ga_sb, gl_sb)):
                    ins = v.tensor_tensor(out=g_lo[b][:, q * P:(q + 1) * P], in0=w[j // 2][:, k, c:c + P],
                                          in1=g_hi[b][:, q * P:(q + 1) * P].bitcast(f32), op=ALU.subtract)
                ins.then_inc(gate_lo, 1)

            def bias_part(j):
                if j == 0:
                    dve.wait_ge(bias_in, 96)
                    then(v.tensor_copy(bias3[0:96, :], bstage[0:96, :]))
                if j == 1:
                    then(v.tensor_tensor(out=bstage[0:96, :], in0=bstage[0:96, :], in1=bias3[0:96, :], op=ALU.subtract))
                if j == 2:
                    v.tensor_copy(bias3[32:64, :], bstage[32:64, :])
                    then(v.tensor_copy(bias3[64:96, :], bstage[64:96, :]))
                if j == 3:
                    then(v.tensor_tensor(out=bstage[64:96, :], in0=bstage[64:96, :], in1=bias3[64:96, :], op=ALU.subtract))
                if j == 4:
                    v.tensor_copy(bias3[64:96, :], bstage[64:96, :]).then_inc(bias_done, 1)
                    dve.wait_ge(bias_done, 1)

            gate_low(0)
            gate_low(1)
            for j in range(KD):
                for n in range(j * KD + 2, min(j * KD + 2 + KD, KD * KD)):
                    gate_low(n)
                bias_part(j)
                for th in range(2):
                    dve.wait_ge(proj_mm, 4 * j + 2 * th + 1)
                    dve.wait_ge(sgate_done, 4 * j + 2 * th + 1)
                    if 2 * j + th >= 1:
                        dve.wait_ge(merged_done, 2 * j + th)
                    v.tensor_tensor(out=part_a, in0=sgate[th][0], in1=bank(4 + 2 * th), op=ALU.mult)
                    dve.wait_ge(proj_mm, 4 * j + 2 * th + 2)
                    dve.wait_ge(sgate_done, 4 * j + 2 * th + 2)
                    then(v.tensor_tensor(out=part_b, in0=sgate[th][1], in1=bank(5 + 2 * th), op=ALU.mult))
                    v.tensor_tensor(out=merged[:, j, th * HALF:(th + 1) * HALF], in0=part_a, in1=part_b,
                                    op=ALU.add).then_inc(merged_done, 1)
            def top(t):
                dve.wait_ge(logit_mm, t + 1)
                v.tensor_tensor(out=logit[:, t, :], in0=bank(6 + t % 2)[:, 0:NE], in1=brt[:], op=ALU.add).then_inc(logit_done, 1)
                dve.wait_ge(logit_done, t + 1)
                then(v.max(top_v[:, t, :], logit[:, t, :]))
                then(v.max_index(top_i[:, t, :], top_v[:, t, :], logit[:, t, :]))

            def wo_low(q):
                half, cols = q // 4, slice((q % 4) * D, (q % 4 + 1) * D)
                dve.wait_ge(wo_hi_done, q + 1)
                v.tensor_tensor(out=wo_lo[half][:, cols], in0=wo_sb[half].rearrange("p k n -> p (k n)")[:, cols],
                                in1=wo_hi[half][:, cols].bitcast(f32), op=ALU.subtract).then_inc(wo_lo_done, 1)

            def merged_low(t):
                dve.wait_ge(m_hi_done, t + 1)
                v.tensor_tensor(out=m_lo[:, :, t * P:(t + 1) * P], in0=merged[:, :, t * P:(t + 1) * P],
                                in1=m_hi[t % 2][:].bitcast(f32), op=ALU.subtract).then_inc(m_lo_done, 1)

            for q in range(4):
                wo_low(q)
            merged_low(0)
            for q in range(4, 8):
                wo_low(q)
            merged_low(1)
            dve.wait_ge(gffn_in, 16)
            for t in range(NT):
                dve.wait_ge(wo_mm, t + 1)
                dve.wait_ge(xb_in[t % 2], 16 * (t // 2 + 1))
                v.tensor_tensor(out=xb[t % 2], in0=bank(2 * (t % 2), 2), in1=xb[t % 2], op=ALU.add).then_inc(x2_done, 1)
                dve.wait_ge(rms_done, NT + t + 1)
                v.reciprocal(rinv[:, 1, t:t + 1], rms[:, 1, t:t + 1]).then_inc(rinv_done, 1)
                dve.wait_ge(rinv_done, NT + t + 1)
                v.scalar_tensor_tensor(out=h2[t % 2], in0=xb[t % 2], scalar=rinv[:, 1, t:t + 1], in1=gffn,
                                       op0=ALU.mult, op1=ALU.mult).then_inc(h2_done, 1)
                if t + 2 < NT:
                    merged_low(t + 2)
                if t >= 2:
                    top(t - 2)
            top(NT - 2)
            top(NT - 1)
            v.tensor_copy(top_f, top_i)
            v.tensor_tensor(out=gate4, in0=top_v[:, :, 0:TOPK], in1=bc(top_v[:, :, 0:1], [P, NT, TOPK]),
                            op=ALU.subtract).then_inc(gexp_in, 1)
            dve.wait_ge(gexp_done, 1)
            then(v.tensor_reduce(out=gsum, in_=gate4, axis=AX, op=ALU.add))
            then(v.reciprocal(gsum, gsum))
            then(v.tensor_tensor(out=gate4, in0=gate4, in1=bc(gsum[:, :, None], [P, NT, TOPK]), op=ALU.mult))
            dve.wait_ge(iota_built, 1)
            for k in range(TOPK):
                then(v.tensor_tensor(out=oh, in0=bc(iota_e[:, None, :], [P, NT, NE]), in1=bc(top_f[:, :, k:k + 1], [P, NT, NE]), op=ALU.is_equal))
                dst = gate_d if k == 0 else ohg
                then(v.tensor_tensor(out=dst, in0=oh, in1=bc(gate4[:, :, k:k + 1], [P, NT, NE]), op=ALU.mult))
                if k == 0:
                    then(v.tensor_copy(mask_d, oh))
                else:
                    v.tensor_tensor(out=mask_d, in0=mask_d, in1=oh, op=ALU.add)
                    then(v.tensor_tensor(out=gate_d, in0=gate_d, in1=ohg, op=ALU.add))
            v.tensor_copy(mask_b, mask_d).then_inc(mask_done, 1)
            mv = meta.rearrange("p (e t c) -> p t e c", e=NE, t=NT)
            v.tensor_copy(mv[:, :, :, 0], bc(iota_t[:, :, None], [P, NT, NE]))
            v.tensor_copy(mv[:, :, :, 1], bc(iota_p[:, :, None], [P, NT, NE]))
            v.memset(mv[:, :, :, 2], -float(FAR))
            then(v.tensor_copy(mv[:, :, :, 3], gate_d))
            then(v.tensor_tensor(out=gate_r, in0=gate_d, in1=mv[:, :, :, 3], op=ALU.subtract))
            then(v.tensor_copy(mv[:, :, :, 4], gate_r))
            then(v.tensor_tensor(out=gate_r, in0=gate_r, in1=mv[:, :, :, 4], op=ALU.subtract))
            then(v.tensor_copy(mv[:, :, :, 5], gate_r))
            dve.wait_ge(rank_mm, 1)
            then(v.scalar_tensor_tensor(out=oh, in0=bank(0)[:, 0:NT * NE].rearrange("p (t e) -> p t e", t=NT), scalar=1.0,
                                        in1=mask_d, op0=ALU.add, op1=ALU.mult))
            then(v.tensor_scalar(rank.rearrange("p e t -> p t e"), oh, -1.0, None, ALU.add))
            then(v.tensor_copy(cnt, bank(1)[:, 0:NE]))
            then(v.memset(nch, 1.0))
            for q in range(1, SEQ // P):
                then(v.scalar_tensor_tensor(out=nch, in0=cnt, scalar=float(P * q), in1=nch, op0=ALU.is_gt, op1=ALU.add))
            then(v.memset(cexc, 0.0))
            then(v.tensor_tensor_scan(cinc, nch, cexc, 0.0, ALU.add, ALU.add))
            then(v.tensor_tensor(out=cexc, in0=cinc, in1=nch, op=ALU.subtract))
            p_ = bc(iota_p, [P, NE])
            then(v.tensor_tensor(out=ended, in0=cinc, in1=p_, op=ALU.is_le))
            then(v.tensor_reduce(out=tab_c[:, 0:1], in_=ended, axis=AX, op=ALU.add))
            then(v.tensor_scalar(tab_c[:, 0:1], tab_c[:, 0:1], float(NE - 1), None, ALU.min))
            then(v.tensor_tensor(out=begun, in0=cexc, in1=p_, op=ALU.is_le))
            then(v.tensor_tensor(out=oh_c, in0=begun, in1=cexc, op=ALU.mult))
            then(v.tensor_reduce(out=tab_c[:, 1:2], in_=oh_c, axis=AX, op=ALU.max))
            then(v.tensor_tensor(out=tab_c[:, 1:2], in0=iota_p, in1=tab_c[:, 1:2], op=ALU.subtract))
            then(v.tensor_scalar(tab_c[:, 1:2], tab_c[:, 1:2], float(NT - 1), None, ALU.min))
            then(v.tensor_tensor(out=begun, in0=begun, in1=ended, op=ALU.subtract))
            then(v.tensor_tensor(out=begun, in0=begun, in1=cnt, op=ALU.mult))
            then(v.tensor_reduce(out=tab_c[:, 2:3], in_=begun, axis=AX, op=ALU.add))
            then(v.scalar_tensor_tensor(out=tab_c[:, 2:3], in0=tab_c[:, 1:2], scalar=-float(P), in1=tab_c[:, 2:3],
                                        op0=ALU.mult, op1=ALU.add))
            then(v.tensor_scalar(tab_c[:, 2:3], tab_c[:, 2:3], float(TAIL), None, ALU.is_le))
            v.scalar_tensor_tensor(out=tab_c[:, 2:3], in0=tab_c[:, 1:2], scalar=1.0, in1=tab_c[:, 2:3],
                                   op0=ALU.is_ge, op1=ALU.mult).then_inc(columns_done, 1)
            dve.wait_ge(columns_mm, 1)
            then(v.tensor_copy(tab_f[:, 0:3, :], bank(1)[0:1, 0:3 * P].rearrange("p (q j) -> p q j", q=3)[:, :, 0:NJ]))
            then(v.tensor_scalar(tab_f[:, 3, :], tab_f[:, 2, :], -1.0, 1.0, ALU.mult, ALU.add))
            then(v.memset(tab_f[:, 4, :], 0.0))
            then(v.tensor_tensor_scan(tab_f[:, 5, :], tab_f[:, 3, :], tab_f[:, 4, :], 0.0, ALU.add, ALU.add))
            then(v.tensor_tensor(out=tab_f[:, 5, :], in0=tab_f[:, 5, :], in1=tab_f[:, 3, :], op=ALU.subtract))
            expert, tile, short, before, both, full = (tab_f[:, q, :] for q in (0, 1, 2, 5, 3, 4))
            later, now = slice(1, NJ), slice(0, MAXC + 1)
            then(v.scalar_tensor_tensor(out=full, in0=both, scalar=4096.0, in1=before, op0=ALU.mult, op1=ALU.add))
            then(v.scalar_tensor_tensor(out=both, in0=short, scalar=32.0, in1=expert, op0=ALU.mult, op1=ALU.add))
            then(v.scalar_tensor_tensor(out=full, in0=full, scalar=64.0, in1=both, op0=ALU.mult, op1=ALU.add))
            then(v.scalar_tensor_tensor(out=full[:, now], in0=both[:, later], scalar=4096.0, in1=full[:, now],
                                        op0=ALU.mult, op1=ALU.add))
            then(v.tensor_copy(step_table[0:1], full))
            then(v.scalar_tensor_tensor(out=both, in0=tile, scalar=32.0, in1=expert, op0=ALU.mult, op1=ALU.add))
            then(v.scalar_tensor_tensor(out=both, in0=short, scalar=256.0, in1=both, op0=ALU.mult, op1=ALU.add))
            then(v.tensor_copy(slot_table[0:1], both))
            v.tensor_copy(ends[:], cinc).then_inc(table_done, 1)

            dve.wait_ge(table_done, 1)
            total = dve.value_load(ends[0:1, NE - 1:NE], min_val=1, max_val=MAXC)

            def slots(e, c, tail):
                of_e = rank[:, ds(e, 1), :].rearrange("p a t -> p (a t)")
                with dve.If(tail < 1):
                    v.tensor_tensor(out=onehot, in0=iota_s[:, ds(c * P, P)][:, None, :].to_broadcast([P, NT, P]),
                                    in1=of_e[:, :, None].to_broadcast([P, NT, P]), op=ALU.is_equal).then_inc(onehot_done, 1)
                with dve.If(tail > 0):
                    for q in range(QUART):
                        ins = v.tensor_tensor(out=onehot[:, :, TAIL * q:TAIL * (q + 1)],
                                              in0=iota_s[:, ds(c * P, TAIL)][:, None, :].to_broadcast([P, NT, TAIL]),
                                              in1=of_e[:, :, None].to_broadcast([P, NT, TAIL]), op=ALU.is_equal)
                    ins.then_inc(onehot_done, 1)

            def selector(u, e):
                v.tensor_copy(sel_cur[0:96, u, :], sel[0:96, ds(e * P, P)]).then_inc(sel_ready, 1)

            N_STEP = 5

            def rows_of(u, base):
                v.tensor_copy(meta_s[:], bank(7)[:, 0:NMETA]).then_inc(dve_step, 1)
                dve.wait_ge(dve_step, base + 1)
                v.tensor_tensor(out=row_f[:, 0:1], in0=meta_s[:, 0:1], in1=meta_s[:, 1:2], op=ALU.add).then_inc(dve_step, 1)
                v.tensor_tensor(out=w_next[:, u, 1:2], in0=meta_s[:, 3:4], in1=meta_s[:, 4:5], op=ALU.add).then_inc(dve_step, 1)
                dve.wait_ge(dve_step, base + 3)
                v.tensor_tensor(out=w_next[:, u, 0:1], in0=w_next[:, u, 1:2], in1=meta_s[:, 5:6], op=ALU.add)
                v.scalar_tensor_tensor(out=row_f[:, 1:2], in0=meta_s[:, 2:3], scalar=float(FAR), in1=row_f[:, 0:1],
                                       op0=ALU.add, op1=ALU.add).then_inc(dve_step, 1)
                dve.wait_ge(dve_step, base + 4)
                v.scalar_tensor_tensor(out=row_f[:, 2:3], in0=row_f[:, 1:2], scalar=float(QUART), in1=quart[:],
                                       op0=ALU.mult, op1=ALU.add).then_inc(dve_step, 1)
                dve.wait_ge(dve_step, base + 5)
                v.tensor_copy(row_next[:, u, :], row_f[:]).then_inc(idx_done, 1)

            def low(n, f):
                i, k0 = sub_unit(n)
                dve.wait_ge(hi_done, f * SUBS + n + 1)
                v.tensor_tensor(out=w_lo[:, n % NBUF, :], in0=place[i][:, k0 * HALF:(k0 + 2) * HALF],
                                in1=w_hi[:, n % NBUF, :].bitcast(f32), op=ALU.subtract).then_inc(lo_dve, 1)

            def rows_low():
                v.tensor_tensor(out=rows_lo[:], in0=bank(6, 2), in1=rows_hi[:].bitcast(f32),
                                op=ALU.subtract).then_inc(rows_lo_done, 1)

            dve.sem_inc(act_done)
            dve.wait_ge(sel_done, 4)
            base0 = steps[0]
            for u in range(2):
                e0, c0, t0 = load_slots(dve, u)
                if u == 1:
                    dve.wait_ge(idx_done, 1)
                slots(e0, c0, t0)
                if u == 0:
                    selector(0, e0)
                dve.wait_ge(meta_mm, u + 1)
                rows_of(u, base0)
                base0 += N_STEP
            dve.wait_ge(rowsT_done, 1)
            rows_low()
            for n in range(NBUF):
                low(n, 0)
            PER = N_STEP + 4
            with dve.Fori(0, MAXC // 2) as pair:
                for u in range(2):
                    j = pair * 2 + u
                    with dve.If(j < total):
                        _, tail, f, e_next, t_next, f_next = load_step(dve, j)
                        e_ahead, c_ahead, t_ahead = load_slots(dve, j + 2)
                        here = j * PER + base0
                        def ahead():
                            wait_reg(dve, meta_mm, j + 2)
                            wait_reg(dve, idx_done, j + 2)
                            slots(e_ahead, c_ahead, t_ahead)
                            wait_reg(dve, y_done, j * 2 + 1)
                            selector(1 - u, e_next)

                        def gate_clip(part, half, b_, signal, clipped):
                            dve.wait_ge(signal, j + 1)
                            dve.wait_ge(act_done, j * 2 + clipped)
                            v.tensor_scalar(part(gclip, half), b_, LIMIT, None, ALU.min).then_inc(gclip_done, 1)

                        def swiglu(part, up, half, b_, signal, step):
                            dve.wait_ge(signal, j + 1)
                            v.tensor_scalar(up, b_, LIMIT, -LIMIT, ALU.min, ALU.max).then_inc(dve_step, 1)
                            dve.wait_ge(gsig_done, j * 2 + half + 1)
                            v.tensor_tensor(out=part(gclip, half), in0=part(gclip, half), in1=part(gsig, half),
                                            op=ALU.mult).then_inc(dve_step, 1)
                            dve.wait_ge(dve_step, step + 2)
                            v.scalar_tensor_tensor(out=up, in0=up, scalar=1.0, in1=part(gclip, half),
                                                   op0=ALU.add, op1=ALU.mult).then_inc(act_done, 1)

                        def next_rows(step):
                            wait_reg(dve, y_done, j * 2 + 1)
                            wait_reg(dve, added, j * 16 + 16)
                            v.tensor_copy(w_cur[:, u:u + 1], w_next[:, u, 0:1])
                            v.tensor_copy(row_cur[:, u, :], row_next[:, u, 1:3]).then_inc(cur_done, 1)
                            wait_reg(dve, meta_mm, j + 3)
                            wait_reg(dve, rows_in[u], (pair + 1) * 16)
                            wait_reg(dve, cur_done, j + 1)
                            rows_of(u, step)

                        def actT_low(half):
                            dve.wait_ge(actT_done, j * 2 + half + 1)
                            v.tensor_tensor(out=act_lo[:, half * HALF:(half + 1) * HALF], in0=bank(2 * half),
                                            in1=act_hi[:, half * HALF:(half + 1) * HALF].bitcast(f32),
                                            op=ALU.subtract).then_inc(act_lo_done, 1)

                        with dve.If(tail < 1):
                            def part(ap, half):
                                return ap

                            for n in range(NBUF, SUBS):
                                if n not in ON_POOL:
                                    low(n, f)
                                if n == 4:
                                    ahead()
                                if n == 7:
                                    gate_clip(part, 0, bank(0), unit_mm[0], 1)
                                if n == 10:
                                    swiglu(part, uclip[:, 0, :], 0, bank(1), unit_mm[1], here)
                                if n == 12:
                                    next_rows(here + 2)
                                if n == 14:
                                    gate_clip(part, 1, bank(2), unit_mm[2], 2)
                                if n == 15:
                                    actT_low(0)
                                if n == 17:
                                    swiglu(part, uclip[:, 1, :], 1, bank(3), unit_mm[3], here + 2 + N_STEP)
                                if n == 21:
                                    actT_low(1)
                        with dve.If(tail > 0):
                            def part(ap, half):
                                return ap[:, half * P:(half + 1) * P]

                            ahead()
                            gate_clip(part, 0, bank(0)[:, 0:P], unit_mm[2], 1)
                            gate_clip(part, 1, bank(0)[:, P:2 * P], unit_mm[2], 1)
                            next_rows(here)
                            swiglu(part, uclip[:, 0, 0:P], 0, bank(1)[:, 0:P], unit_mm[3], here + N_STEP)
                            swiglu(part, uclip[:, 0, P:2 * P], 1, bank(1)[:, P:2 * P], unit_mm[3], here + N_STEP + 2)
                        with dve.If(t_next < 1):
                            dve.wait_ge(rowsT_done, j + 2)
                            rows_low()
                            for n in range(NBUF):
                                low(n, f_next)
            for t in range(NT):
                dve.wait_ge(frms, t + 1)
                v.reciprocal(rinv[:, 2, t:t + 1], rms[:, 2, t:t + 1]).then_inc(frinv, 1)
                dve.wait_ge(frinv, t + 1)
                v.scalar_tensor_tensor(out=fin[t], in0=fin[t], scalar=rinv[:, 2, t:t + 1], in1=gfin,
                                       op0=ALU.mult, op1=ALU.mult).then_inc(fin_done, 1)


_INS = ["x", "positions", "norm_mix_g", "w_in", "conv_w", "conv_b", "w_rg", "b_rg", "w_ig", "b_ig", "lru_lambda",
        "attn_sinks", "w_attn_o", "w_lru_o", "w_out", "norm_ffn_g", "w_router", "b_router", "w_gate_up", "b_gate_up",
        "w_down", "b_down", "norm_final_g"]


def kernel(**inputs):
    import numpy as _np
    import concourse.bacc as _bacc
    from concourse import mybir as _mybir
    from concourse.bass_utils import run_bass_kernel_spmd as _run

    nc = _bacc.Bacc("TRN2", target_bir_lowering=False, num_devices=1)
    arrays, args = {}, []
    for name in _INS:
        a = _np.ascontiguousarray(inputs[name])
        arrays[f"in_{name}_dram"] = a
        args.append(nc.dram_tensor(f"in_{name}_dram", a.shape, _mybir.dt.from_np(a.dtype), kind="ExternalInput").ap())
    half = HD // 2
    freq = (_np.float32(1.0) / (_np.float32(10000.0) ** (_np.arange(0, HD, 2, dtype=_np.float32) / _np.float32(HD)))).astype(_np.float32)
    assert freq.shape == (half,)
    arrays["in_inv_freq_dram"] = freq
    args.append(nc.dram_tensor("in_inv_freq_dram", freq.shape, _mybir.dt.float32, kind="ExternalInput").ap())
    args.append(nc.dram_tensor("out_0_dram", (1, SEQ, D), _mybir.dt.float32, kind="ExternalOutput").ap())
    hybrid_decoder_block(nc, *args)
    r = _run(nc, [arrays], core_ids=[0])
    return r.results[0]["out_0_dram"]
```
